# Optimizing a Trainium2 kernel written in Bass

```python
import math
import jax, jax.numpy as jnp
from jax import lax
import numpy as np

D_MODEL = 1024
BATCH = 1
SEQ = 1024
DEPTH = 1

D_CONV = D_MODEL
CONV_K = 3
HEAD_DIM = 64
N_HEADS = 16
N_KV_HEADS = 4
GROUP = N_HEADS // N_KV_HEADS
D_ATTN = N_HEADS * HEAD_DIM
D_KV = N_KV_HEADS * HEAD_DIM
WINDOW = 128
BLOCK = 128
ROT_DIM = HEAD_DIM // 4
ROPE_THETA = 500000.0
ATTN_SCALE = 1.0 / math.sqrt(HEAD_DIM)
NEG_INF = -1e30
D_FF = ((8 * D_MODEL // 3 + 255) // 256) * 256
EPS = 1e-5

IN_WIDTHS = (D_CONV, D_CONV, D_CONV, D_ATTN, D_KV, D_KV, D_MODEL, D_MODEL)
N_IN = sum(IN_WIDTHS)
SPLIT_POINTS = tuple(int(v) for v in np.cumsum(IN_WIDTHS)[:-1])

kernel_name = "hybrid_gated_conv_swa_sink_block"

def rms_norm(x, g):
    xf = x.astype(jnp.float32)
    y = xf * lax.rsqrt(jnp.mean(xf * xf, axis=-1, keepdims=True) + EPS)
    return (y * g.astype(jnp.float32)).astype(x.dtype)

def rotary_tables(seq, dtype):
    inv_freq = ROPE_THETA ** (-jnp.arange(0, ROT_DIM, 2, dtype=jnp.float32) / ROT_DIM)
    ang = jnp.arange(seq, dtype=jnp.float32)[:, None] * inv_freq[None, :]
    return jnp.cos(ang).astype(dtype), jnp.sin(ang).astype(dtype)

def partial_rotary(t, cos, sin):
    rot, rest = t[..., :ROT_DIM], t[..., ROT_DIM:]
    r1, r2 = rot[..., :ROT_DIM // 2], rot[..., ROT_DIM // 2:]
    c = cos[None, :, None, :]
    s = sin[None, :, None, :]
    rot = jnp.concatenate([r1 * c - r2 * s, r2 * c + r1 * s], axis=-1)
    return jnp.concatenate([rot, rest], axis=-1)

def causal_depthwise_conv(u, w):
    rhs = w[:, None, :].astype(u.dtype)
    return lax.conv_general_dilated(
        u, rhs, window_strides=(1,), padding=[(CONV_K - 1, 0)],
        dimension_numbers=('NWC', 'WIO', 'NWC'), feature_group_count=u.shape[-1])

def sliding_window_sink_attention(q, k, v, sinks):
    b, s = q.shape[0], q.shape[1]
    nb = s // BLOCK
    qb = q.reshape(b, nb, BLOCK, N_KV_HEADS, GROUP, HEAD_DIM)

    def band(t):
        tp = jnp.pad(t, ((0, 0), (BLOCK, 0), (0, 0), (0, 0)))
        tp = tp.reshape(b, nb + 1, BLOCK, N_KV_HEADS, HEAD_DIM)
        return jnp.concatenate([tp[:, :-1], tp[:, 1:]], axis=2)

    kb, vb = band(k), band(v)
    scores = jnp.einsum('bnqhgd,bnkhd->bnhgqk', qb, kb,
                        preferred_element_type=jnp.float32) * ATTN_SCALE
    qi = jnp.arange(BLOCK)[:, None]
    kj = jnp.arange(2 * BLOCK)[None, :]
    rel = qi + BLOCK - kj
    in_window = (rel >= 0) & (rel < WINDOW)
    key_pos = jnp.arange(nb)[:, None] * BLOCK - BLOCK + jnp.arange(2 * BLOCK)[None, :]
    mask = in_window[None] & (key_pos >= 0)[:, None, :]
    scores = jnp.where(mask[None, :, None, None], scores, NEG_INF)
    sink = jnp.broadcast_to(sinks.astype(jnp.float32).reshape(1, 1, N_KV_HEADS, GROUP, 1, 1),
                            scores.shape[:-1] + (1,))
    probs = jax.nn.softmax(jnp.concatenate([scores, sink], axis=-1), axis=-1)[..., :-1]
    out = jnp.einsum('bnhgqk,bnkhd->bnqhgd', probs.astype(v.dtype), vb)
    return out.reshape(b, s, D_ATTN)

def setup_inputs(seed: int = 0) -> dict:
    key = jax.random.key(seed)
    ks = jax.random.split(key, 13)
    f32 = jnp.float32

    def w(k, shape, fan_in):
        return jax.random.normal(k, shape, f32) * (fan_in ** -0.5)

    def gain(k, shape):
        return 1.0 + 0.05 * jax.random.normal(k, shape, f32)

    return {
        "x": jax.random.normal(ks[0], (BATCH, SEQ, D_MODEL), f32),
        "g_mix": gain(ks[1], (DEPTH, D_MODEL)),
        "w_in": w(ks[2], (DEPTH, D_MODEL, N_IN), D_MODEL),
        "conv_w": w(ks[3], (DEPTH, CONV_K, D_CONV), CONV_K),
        "attn_sinks": 0.5 * jax.random.normal(ks[4], (DEPTH, N_HEADS), f32),
        "w_conv_out": w(ks[5], (DEPTH, D_CONV, D_MODEL), D_CONV),
        "w_attn_out": w(ks[6], (DEPTH, D_ATTN, D_MODEL), D_ATTN),
        "w_o": w(ks[7], (DEPTH, D_MODEL, D_MODEL), D_MODEL),
        "g_ffn": gain(ks[8], (DEPTH, D_MODEL)),
        "w_gate_up": w(ks[9], (DEPTH, D_MODEL, 2 * D_FF), D_MODEL),
        "w_down": w(ks[10], (DEPTH, D_FF, D_MODEL), D_FF),
        "g_final": gain(ks[11], (D_MODEL,)),
    }

def reference(x, g_mix, w_in, conv_w, attn_sinks, w_conv_out, w_attn_out, w_o,
              g_ffn, w_gate_up, w_down, g_final):
    b, s, _ = x.shape
    cos, sin = rotary_tables(s, x.dtype)
    for l in range(DEPTH):
        h = rms_norm(x, g_mix[l])
        proj = jnp.einsum('bsd,dn->bsn', h, w_in[l])
        cb, cc, cx, q, k, v, gate_c, gate_a = jnp.split(proj, SPLIT_POINTS, axis=-1)

        conv_y = cb * causal_depthwise_conv(cc * cx, conv_w[l])
        conv_out = jnp.einsum('bsc,cd->bsd', conv_y, w_conv_out[l])

        q = partial_rotary(q.reshape(b, s, N_HEADS, HEAD_DIM), cos, sin)
        k = partial_rotary(k.reshape(b, s, N_KV_HEADS, HEAD_DIM), cos, sin)
        v = v.reshape(b, s, N_KV_HEADS, HEAD_DIM)
        attn = sliding_window_sink_attention(q, k, v, attn_sinks[l])
        attn_out = jnp.einsum('bsc,cd->bsd', attn, w_attn_out[l])

        merged = jax.nn.sigmoid(gate_c) * conv_out + jax.nn.sigmoid(gate_a) * attn_out
        x = x + jnp.einsum('bsd,de->bse', merged, w_o[l])

        h = rms_norm(x, g_ffn[l])
        gu = jnp.einsum('bsd,df->bsf', h, w_gate_up[l])
        g_act, up = gu[..., :D_FF], gu[..., D_FF:]
        x = x + jnp.einsum('bsf,fd->bsd', jax.nn.silu(g_act) * up, w_down[l])
    return rms_norm(x, g_final)


_drawn_inputs = setup_inputs


def setup_inputs(seed=0):
    import zlib

    import numpy as np

    out = dict(_drawn_inputs(seed))
    spreads = {}
    factors = {'attn_sinks': 8.0}
    for name, (base, spread) in spreads.items():
        noise = np.random.default_rng([zlib.crc32(name.encode()), seed]).standard_normal(out[name].shape)
        drawn = base * np.exp(spread * noise) if base else spread * noise
        out[name] = __import__('jax').numpy.asarray(drawn.astype(out[name].dtype))
    for name, factor in factors.items():
        out[name] = (out[name] * factor).astype(out[name].dtype)
    return out
```

```python
from contextlib import ExitStack, contextmanager

import numpy as np

import concourse.bass as bass
from concourse import mybir

F32 = mybir.dt.float32
F32R = mybir.dt.float32r
U8 = mybir.dt.uint8
ALU = mybir.AluOpType
ACT = mybir.ActivationFunctionType
AX = mybir.AxisListType

P = 128
D = 1024
S = 1024
KT = D // P
HALF = 512
HEAD = 64
N_HEADS = 16
N_KV = 4
GROUP = N_HEADS // N_KV
PAIRS = N_KV // 2
NB = S // P
UNITS = PAIRS * NB
D_FF = ((8 * D // 3 + 255) // 256) * 256
FT = D_FF // P
CHUNKS = (8, 8, 6)
ROT = HEAD // 4
SCALE = float(HEAD) ** -0.5
EPS = 1e-5
NEG = -1e30

T_V = 0
T_K = T_V + PAIRS
T_Q = T_K + PAIRS
T_GATE = T_Q + KT
T_CONV = T_GATE + 2 * KT
T_CO = T_CONV + 3 * KT
T_AO = T_CO + KT
T_WO = T_AO + KT
T_UP = []
T_DOWN = []
_t = T_WO + KT
for _f in CHUNKS:
    T_UP.append(_t)
    T_DOWN.append(_t + 2 * _f)
    _t += 2 * _f + KT
TILES = _t
assert sum(CHUNKS) == FT and TILES % 2 == 0


@contextmanager
def by_two(engine, first, last):
    with engine.Fori(0, (last - first) // 2) as i:
        yield i * 2 + first


def block_kernel(nc, x_t, w_stream, gains, conv_w, sinks, out_t, consts, gate_scratch):
    with ExitStack() as ctx:
        def sb(name, shape, dt=F32):
            return ctx.enter_context(nc.sbuf_tensor(name, shape, dt))

        def sem(name):
            return ctx.enter_context(nc.semaphore(name))

        def psum(name, shape):
            return ctx.enter_context(nc.psum_tensor(name, shape, F32))

        w_raw = [sb(f"w_raw{i}", [P, KT * P]) for i in range(2)]
        w_hi = [sb(f"w_hi{i}", [P, KT * P], F32R) for i in range(2)]
        w_lo = [sb(f"w_lo{i}", [P, KT * P], F32R) for i in range(2)]
        h_at = nc.sbuf_base
        h_hi = sb("h_hi", [P, KT, S], F32R)
        h_lo = sb("h_lo", [P, KT, S], F32R)
        m = sb("m", [P, KT * S])
        rstd = sb("rstd", [P, S])
        rstd_sq = sb("rstd_sq", [P, S])
        work_a = sb("work_a", [P, S])
        work_b_at = nc.sbuf_base
        work_b = sb("work_b", [P, S + 8])
        work_c_at = nc.sbuf_base
        work_c = sb("work_c", [P, S])
        ident = sb("ident", [P, P])
        mean_w = sb("mean_w", [P, P], F32R)
        keep_cur = sb("keep_cur", [P, P])
        take_cur = sb("take_cur", [P, GROUP * P], U8)
        bias_table = sb("bias_table", [P, 2 * UNITS + 1])
        prev_bias = sb("prev_bias", [P, 1])
        zero = sb("zero", [P, 1])
        gain = sb("gain", [P, 3 * KT])
        taps = sb("taps", [P, 3 * KT])
        sink = sb("sink", [P, 2 * UNITS * GROUP])
        eps = sb("eps", [P, 1])
        row_max = sb("row_max", [P, GROUP])
        top = sb("top", [P, GROUP])
        neg_max = sb("neg_max", [P, GROUP])
        sink_arg = sb("sink_arg", [P, GROUP])
        sink_exp = sb("sink_exp", [P, GROUP])
        exp_sum = sb("exp_sum", [P, GROUP])
        denom = sb("denom", [P, GROUP])
        inv_denom = sb("inv_denom", [P, GROUP])

        with ExitStack() as attention_only:
            def asb(name, shape, dt=F32):
                return attention_only.enter_context(nc.sbuf_tensor(name, shape, dt))

            rope_cos = asb("rope_cos", [P, S])
            rope_sin = asb("rope_sin", [P, S])
            keys = asb("keys", [P, (UNITS + 1) * P])
            values = asb("values", [P, (UNITS + 1) * P])
            with ExitStack() as before_attention:
                v_feature = [before_attention.enter_context(nc.sbuf_tensor(f"v_feature{i}", [P, S], F32))
                             for i in range(PAIRS)]
            q_hi = [asb(f"q_hi{i}", [P, GROUP * P], F32R) for i in range(2)]
            q_lo = [asb(f"q_lo{i}", [P, GROUP * P], F32R) for i in range(2)]
            k_hi = [asb(f"k_hi{i}", [P, 2 * P], F32R) for i in range(2)]
            k_lo = [asb(f"k_lo{i}", [P, 2 * P], F32R) for i in range(2)]
            v_hi = [asb(f"v_hi{i}", [P, 2 * P], F32R) for i in range(2)]
            v_lo = [asb(f"v_lo{i}", [P, 2 * P], F32R) for i in range(2)]
            scores = asb("scores", [P, GROUP, P])
            prob = asb("prob", [P, GROUP, P])
            pt_cur = asb("pt_cur", [P, GROUP, P])
            pt_prev = asb("pt_prev", [P, GROUP, P])
            pt_hi = [asb(f"pt_hi{i}", [P, GROUP * P], F32R) for i in range(2)]
            pt_lo = [asb(f"pt_lo{i}", [P, GROUP * P], F32R) for i in range(2)]
        c_hi = sb("c_hi", [P, KT, S], F32R)
        c_lo = sb("c_lo", [P, KT, S], F32R)
        ssq_hi = nc.alloc_sbuf_tensor_at("ssq_hi", [P, S], F32R, offset=work_b_at)
        ssq_lo = nc.alloc_sbuf_tensor_at("ssq_lo", [P, S], F32R, offset=work_c_at)
        y = nc.alloc_sbuf_tensor_at("y", [P, KT, S], F32, offset=h_at)

        slot_ps = [psum(f"slot_ps{i}", [P, S]) for i in range(2)]
        scores_ps = psum("scores_ps", [P, S])
        spare_ps = psum("spare_ps", [P, S])
        turn_ps = spare_ps[:, 0:GROUP * P]
        attn_ps = spare_ps[:, GROUP * P:2 * GROUP * P]

        def feature_tile(kt):
            pair, head = kt // GROUP, kt % GROUP
            v = m[:].rearrange("p (a b t q) -> p a b t q", a=PAIRS, b=NB, t=GROUP)
            return v[:, pair, :, head, :]

        def blocks(ap):
            return ap.rearrange("p (b q) -> p b q", b=NB)

        def residual(n):
            return m[:, n * S:(n + 1) * S]

        gains_loaded = sem("gains_loaded")
        consts_loaded = sem("consts_loaded")
        x_loaded = [sem(f"x_loaded{k}") for k in range(KT)]
        raw_loaded = [sem(f"raw_loaded{i}") for i in range(2)]
        raw_hi = sem("raw_hi")
        weights_split = sem("weights_split")
        setup_done = sem("setup_done")
        tile_done = sem("tile_done")
        psum_read = sem("psum_read")
        h_hi_ready = sem("h_hi_ready")
        h_lo_ready = sem("h_lo_ready")
        c_hi_ready = sem("c_hi_ready")
        c_lo_ready = sem("c_lo_ready")
        square_ready = sem("square_ready")
        square_added = sem("square_added")
        ssq_split = sem("ssq_split")
        mean_done = sem("mean_done")
        rms_ready = sem("rms_ready")
        rstd_ready = sem("rstd_ready")
        rstd_sq_ready = sem("rstd_sq_ready")
        swapped = sem("swapped")
        cos_part = sem("cos_part")
        sin_part = sem("sin_part")
        roped = sem("roped")
        v_turned = sem("v_turned")
        v_stored = sem("v_stored")
        unit_hi = sem("unit_hi")
        unit_lo = sem("unit_lo")
        scores_done = sem("scores_done")
        mask_ready = sem("mask_ready")
        bias_set = sem("bias_set")
        prev_copied = sem("prev_copied")
        scores_merged = sem("scores_merged")
        max_ready = sem("max_ready")
        top_ready = sem("top_ready")
        shift_ready = sem("shift_ready")
        sink_arg_ready = sem("sink_arg_ready")
        exp_done = sem("exp_done")
        denom_ready = sem("denom_ready")
        inv_ready = sem("inv_ready")
        probs_ready = sem("probs_ready")
        probs_turned = sem("probs_turned")
        pt_masked = sem("pt_masked")
        pt_hi_ready = sem("pt_hi_ready")
        pt_lo_ready = sem("pt_lo_ready")
        pv_done = sem("pv_done")
        attn_stored = sem("attn_stored")
        gate_tanh = sem("gate_tanh")
        gate_stored = [sem(f"gate_stored{i}") for i in range(2)]
        gate_loaded = [sem(f"gate_loaded{i}") for i in range(2)]
        conv_tap = sem("conv_tap")
        conv_gated = sem("conv_gated")
        branches_added = sem("branches_added")
        x_reloaded = [sem(f"x_reloaded{i}") for i in range(2)]
        silu_tanh = sem("silu_tanh")
        silu_gate = sem("silu_gate")
        ffn_act = sem("ffn_act")
        y_scaled = sem("y_scaled")
        out_dve = sem("out_dve")
        out_pool = sem("out_pool")
        out_stored = sem("out_stored")

        N_CONSTS = len(consts) + 2
        POOL_OUT = 3
        gate_buf = [work_b, work_c]
        square_buf = [work_a, work_b]
        reload_buf = [work_a, work_b]

        block = ctx.enter_context(nc.Block())

        @block.sync
        def _(sp):
            def load_weights(t_expr, slot, count, first=False):
                if not first:
                    sp.wait_ge(weights_split, count)
                sp.dma_start(w_raw[slot][:], w_stream[bass.ds(t_expr, 1), :, :].rearrange("a p n -> (a p) n")
                             ).then_inc(raw_loaded[slot], 16)

            load_weights(0, 0, 0, first=True)
            sp.wait_ge(x_loaded[KT // 2], 16)
            load_weights(1, 1, 0, first=True)
            sp.wait_ge(x_loaded[KT - 1], 16)
            for dst, src in ((taps, conv_w), (sink, sinks), (ident, consts["ident"]),
                             (keep_cur, consts["keep_cur"]),
                             (prob[:, 0, :], consts["take_cur"]), (bias_table, consts["bias_table"]),
                             (rope_cos, consts["rope_cos"]), (rope_sin, consts["rope_sin"])):
                sp.dma_start(dst[:], src).then_inc(consts_loaded, 16)
            with by_two(sp, 2, T_CO + 2) as t:
                for j in range(2):
                    load_weights(t + j, j, t + (j - 1))
            for i in range(2):
                sp.wait_ge(gate_stored[i], 16 * KT)
            sp.wait_ge(conv_gated, KT)
            sp.wait_ge(conv_tap, 3 * KT)

            def reload(j, t, n, source, done):
                sp.wait_ge(psum_read, t - 1)
                sp.dma_start(reload_buf[j][:, 0:S], source[bass.ds(n, 1), :, :].rearrange("a p n -> (a p) n")
                             ).then_inc(done[j], 16)
                load_weights(t + 2, j, t + 1)

            with by_two(sp, 0, 2 * KT) as n:
                for j in range(2):
                    reload(j, n + (T_CO + j), n + j, gate_scratch, gate_loaded)
            with by_two(sp, 0, KT) as n:
                for j in range(2):
                    reload(j, n + (T_WO + j), n + j, x_t, x_reloaded)
            with by_two(sp, T_UP[0] + 2, TILES) as t:
                for j in range(2):
                    load_weights(t + j, j, t + (j - 1))
            for n in range(KT):
                if n < KT - POOL_OUT:
                    sp.wait_ge(out_dve, n + 1)
                else:
                    sp.wait_ge(out_pool, n - (KT - POOL_OUT) + 1)
                sp.dma_start(out_t[n], y[:, n, :]).then_inc(out_stored, 16)
            sp.wait_ge(out_stored, 16 * KT)

        @block.gpsimd
        def _(pool):
            pool.memset(zero[:], 0.0).then_inc(setup_done, 1)
            pool.memset(mean_w[:].bitcast(F32), 1.0 / D).then_inc(setup_done, 1)
            pool.memset(eps[:], EPS).then_inc(setup_done, 1)
            pool.memset(keys[:, 0:P], 0.0).then_inc(setup_done, 1)
            pool.memset(values[:, 0:P], 0.0).then_inc(setup_done, 1)

            def split(slot, loads, t_plus_1, first):
                pool.wait_ge(raw_loaded[slot], loads)
                if not first:
                    pool.wait_ge(tile_done, t_plus_1 - 2)
                nc.gpsimd.tensor_tensor(w_hi[slot][:], w_raw[slot][:], zero[:].to_broadcast([P, KT * P]),
                                        ALU.add).then_inc(raw_hi, 1)
                pool.wait_ge(raw_hi, t_plus_1)
                nc.gpsimd.tensor_tensor(w_lo[slot][:], w_raw[slot][:], w_hi[slot][:].bitcast(F32),
                                        ALU.subtract).then_inc(weights_split, 1)

            pool.wait_ge(setup_done, 1)
            for j in range(2):
                split(j, 16, j + 1, True)
            with pool.Fori(1, TILES // 2) as i:
                for j in range(2):
                    split(j, i * 16 + 16, i * 2 + (j + 1), False)
            pool.wait_ge(rstd_ready, 3)
            for n in range(KT - POOL_OUT, KT):
                pool.wait_ge(y_scaled, n + 1)
                nc.gpsimd.tensor_tensor(y[:, n, :], y[:, n, :], rstd[:], ALU.mult).then_inc(out_pool, 1)

        @block.tensor
        def _(pe):
            def product(slot, rhs_hi, rhs_lo, k_tiles=KT, halves=(0, 1), ready=None, between=None,
                        ps=None):
                ps = slot_ps[slot] if ps is None else ps
                last = None
                for k in range(k_tiles):
                    if ready is not None:
                        pe.wait_ge(ready[0], ready[2] + k + 1)
                        pe.wait_ge(ready[1], ready[2] + k + 1)
                    for i, (w, r) in enumerate(((w_hi, rhs_hi), (w_hi, rhs_lo), (w_lo, rhs_hi))):
                        for s in halves:
                            cols = slice(s * HALF, (s + 1) * HALF)
                            last = nc.tensor.matmul(ps[:, cols], w[slot][:, k * P:(k + 1) * P],
                                                    r[:, k, cols], start=(k == 0 and i == 0),
                                                    stop=(k == k_tiles - 1 and i == 2))
                    if between is not None and between[0] == k:
                        between[1]()
                return last

            def slot_free(t_minus_1):
                pe.wait_ge(psum_read, t_minus_1)

            def tile(t, slot, rhs, **how):
                pe.wait_ge(weights_split, t + 1)
                if not isinstance(t, int) or t >= 3:
                    slot_free(t + (-1))
                product(slot, *rhs, **how).then_inc(tile_done, 1)

            def tiles(first, last, rhs, k_tiles=KT, ready=None):
                with by_two(pe, first, last) as t:
                    tile(t, 0, rhs, k_tiles=k_tiles, ready=ready)
                    tile(t + 1, 1, rhs, k_tiles=k_tiles)

            def mean_square(n):
                pe.wait_ge(ssq_split, 2 * n)
                for s in range(2):
                    cols = slice(s * HALF, (s + 1) * HALF)
                    nc.tensor.matmul(scores_ps[:, cols], mean_w[:], ssq_hi[:, cols], start=True, stop=False)
                    last = nc.tensor.matmul(scores_ps[:, cols], mean_w[:], ssq_lo[:, cols],
                                            start=False, stop=True)
                last.then_inc(mean_done, 1)

            def turn_values(i):
                pe.wait_ge(psum_read, T_V + i + 1)
                if i:
                    pe.wait_ge(v_stored, i)
                else:
                    pe.wait_ge(rms_ready, 1)
                for b in range(NB):
                    last = nc.tensor.transpose(scores_ps[:, b * P:(b + 1) * P],
                                               v_feature[i][:, b * P:(b + 1) * P], ident[:])
                last.then_inc(v_turned, 1)

            H = (h_hi, h_lo)
            C = (c_hi, c_lo)
            tile(0, 0, H, ready=(h_hi_ready, h_lo_ready, 0))
            tile(1, 1, H, between=(6, lambda: mean_square(1)))
            tile(2, 0, H, ps=spare_ps)
            tile(3, 1, H)
            pe.wait_ge(consts_loaded, 16 * N_CONSTS)
            tile(4, 0, H, between=(4, lambda: turn_values(0)))
            tile(5, 1, H, between=(4, lambda: turn_values(1)))
            tiles(6, T_GATE, H)

            def score(n, par, h):
                u = n * 2 + h
                if h == 0:
                    pe.wait_ge(unit_hi, n * 3 + 3)
                    pe.wait_ge(unit_lo, n * 3 + 3)
                if not isinstance(u, int) or u > 0:
                    pe.wait_ge(scores_merged, u)
                rows = slice(h * HEAD, (h + 1) * HEAD)
                for t in range(GROUP):
                    dst = scores_ps[:, t * 2 * P:(t + 1) * 2 * P]
                    q_cols = slice(t * P, (t + 1) * P)
                    for i, (q, k) in enumerate(((q_hi, k_hi), (q_lo, k_hi), (q_hi, k_lo))):
                        last = nc.tensor.matmul(dst, q[par][rows, q_cols], k[par][rows, :],
                                                start=(i == 0), stop=(i == 2))
                last.then_inc(scores_done, 1)

            def turn_probs(u):
                pe.wait_ge(probs_ready, u + 1)
                if not isinstance(u, int) or u > 0:
                    pe.wait_ge(pt_masked, u * 2)
                for t in range(GROUP):
                    last = nc.tensor.transpose(turn_ps[:, t * P:(t + 1) * P], prob[:, t, :], ident[:])
                last.then_inc(probs_turned, 1)

            def weigh_values(par, u):
                pe.wait_ge(pt_hi_ready, u * 2 + 2)
                pe.wait_ge(pt_lo_ready, u * 2 + 2)
                if not isinstance(u, int) or u > 0:
                    pe.wait_ge(attn_stored, u)
                n = 0
                for which, v_cols in ((0, slice(P, 2 * P)), (1, slice(0, P))):
                    for v, p in ((v_hi, pt_hi), (v_lo, pt_hi), (v_hi, pt_lo)):
                        last = nc.tensor.matmul(attn_ps, v[par][:, v_cols], p[which][:],
                                                start=(n == 0), stop=(n == 5))
                        n += 1
                last.then_inc(pv_done, 1)

            def attention_step(n, par, h, first=False):
                u = n * 2 + h
                score(n, par, h)
                if not first:
                    turn_probs(u - 1)
                if h == 0:
                    pe.wait_ge(weights_split, n + (T_GATE + 1))
                    slot_free(n + (T_GATE - 1))
                done = product(par, *H, halves=(h,))
                if h == 1:
                    done.then_inc(tile_done, 1)
                if not first:
                    weigh_values(par if h == 1 else 1 - par, u - 1)

            for n in range(2):
                for h in range(2):
                    attention_step(n, n, h, first=(n == 0 and h == 0))
            with by_two(pe, 2, UNITS) as n:
                for par in range(2):
                    for h in range(2):
                        attention_step(n + par, par, h)
            turn_probs(2 * UNITS - 1)
            tile(T_CONV, 0, H)
            weigh_values(1, 2 * UNITS - 1)
            tile(T_CONV + 1, 1, H)
            tiles(T_CONV + 2, T_CO, H)
            tiles(T_CO, T_AO, C, ready=(c_hi_ready, c_lo_ready, 0))
            tiles(T_AO, T_WO, H, ready=(h_hi_ready, h_lo_ready, KT))
            tiles(T_WO, T_UP[0], C, ready=(c_hi_ready, c_lo_ready, KT))
            c_base = 2 * KT
            for c, width in enumerate(CHUNKS):
                if c == 0:
                    tile(T_UP[0], 0, H, ready=(h_hi_ready, h_lo_ready, 2 * KT))
                    tile(T_UP[0] + 1, 1, H, between=(1, lambda: mean_square(2)))
                    tiles(T_UP[0] + 2, T_DOWN[0], H)
                else:
                    tiles(T_UP[c], T_DOWN[c], H)
                tiles(T_DOWN[c], T_DOWN[c] + KT, C, k_tiles=width, ready=(c_hi_ready, c_lo_ready, c_base))
                c_base += width
            mean_square(3)

        @block.scalar
        def _(act):
            act.dma_start(gain[:], gains).then_inc(gains_loaded, 16)
            for k in range(KT):
                act.dma_start(residual(k), x_t[k]).then_inc(x_loaded[k], 16)

            def copy(dst, src, done):
                return nc.scalar.activation(dst, src, ACT.Copy).then_inc(done, 1)

            act.wait_ge(gains_loaded, 16)
            for k in range(KT):
                act.wait_ge(x_loaded[k], 16)
                nc.scalar.activation(h_hi[:, k, :], residual(k), ACT.Copy, scale=gain[:, k:k + 1]
                                     ).then_inc(h_hi_ready, 1)

            def rms(n):
                act.wait_ge(square_added, n * KT)
                copy(ssq_hi[:], rstd_sq[:], ssq_split)
                act.wait_ge(mean_done, n)
                nc.scalar.activation(rstd[:], scores_ps[:], ACT.Sqrt, bias=eps[:]).then_inc(rms_ready, 1)

            act.wait_ge(setup_done, 5)
            for k in range(KT):
                if k >= 2:
                    act.wait_ge(square_added, k - 1)
                nc.scalar.activation(square_buf[k % 2][:, 0:S], residual(k), ACT.Square
                                     ).then_inc(square_ready, 1)
            rms(1)
            for i in range(PAIRS):
                act.wait_ge(v_turned, i + 1)
                copy(values[:, P + i * S:P + (i + 1) * S], scores_ps[:], v_stored)

            def split_unit(n, par, first=False):
                if not first:
                    act.wait_ge(pv_done, n * 2 + (-2))
                copy(q_hi[par][:], m[:, bass.ds(n * (GROUP * P), GROUP * P)], unit_hi)
                copy(k_hi[par][:], keys[:, bass.ds(n * P, 2 * P)], unit_hi)
                copy(v_hi[par][:], values[:, bass.ds(n * P, 2 * P)], unit_hi)

            act.wait_ge(mask_ready, 1)

            def softmax(u, before_exp=None):
                act.wait_ge(scores_done, u + 1)
                if not isinstance(u, int) or u > 0:
                    act.wait_ge(exp_done, u * (GROUP + 1))
                act.wait_ge(bias_set, u + 1)
                by_head = scores_ps[:].rearrange("p (t w k) -> p t w k", t=GROUP, w=2)
                nc.scalar.activation(scores[:], by_head[:, :, 0, :], ACT.Identity,
                                     bias=prev_bias[:]).then_inc(prev_copied, 1)
                if before_exp is not None:
                    before_exp()
                act.wait_ge(shift_ready, u + 1)
                if not isinstance(u, int) or u > 0:
                    act.wait_ge(probs_turned, u)
                    act.wait_ge(denom_ready, u)
                for t in range(GROUP):
                    nc.scalar.activation(prob[:, t, :], scores[:, t, :], ACT.Exp, bias=neg_max[:, t:t + 1],
                                         scale=SCALE, accum_out=exp_sum[:, t:t + 1]).then_inc(exp_done, 1)
                act.wait_ge(sink_arg_ready, u + 1)
                nc.scalar.activation(sink_exp[:], sink_arg[:], ACT.Exp).then_inc(exp_done, 1)

            def pt_high(u):
                if not isinstance(u, int) or u > 0:
                    act.wait_ge(pv_done, u)
                for i, pt in enumerate((pt_cur, pt_prev)):
                    act.wait_ge(pt_masked, u * 2 + (i + 1))
                    copy(pt_hi[i][:], pt[:].rearrange("p t q -> p (t q)"), pt_hi_ready)

            def gate(n, par, first):
                act.wait_ge(psum_read, n + (T_GATE + 1))
                if not first:
                    act.wait_ge(gate_stored[par], n * 8 + (-8 * par))
                nc.scalar.activation(gate_buf[par][:, 0:S], work_a[:], ACT.Tanh, scale=0.5
                                     ).then_inc(gate_tanh, 1)
                act.wait_ge(gate_tanh, n + 1)
                act.dma_start(gate_scratch[bass.ds(n, 1), :, :].rearrange("a p n -> (a p) n"),
                              gate_buf[par][:, 0:S]).then_inc(gate_stored[par], 16)

            def step(n, par, h, first=False, second=False, last=False):
                u = n * 2 + h

                def for_others():
                    if not first:
                        pt_high(u - 1)
                    if h == 1 and not last:
                        split_unit(n + 1, 1 - par, first=(isinstance(n, int) and n == 0))

                softmax(u, before_exp=for_others)
                if h == 0 and not first:
                    gate(n - 1, 1 - par, first=second)

            act.wait_ge(roped, PAIRS + GROUP)
            act.wait_ge(v_stored, PAIRS)
            split_unit(0, 0, first=True)
            for n in range(4):
                for h in range(2):
                    if (n, h) == (0, 1):
                        act.wait_ge(roped, PAIRS + KT)
                    step(n, n % 2, h, first=(n == 0 and h == 0), second=(n in (1, 2)))
            with by_two(act, 4, UNITS - 2) as n:
                for par in range(2):
                    for h in range(2):
                        step(n + par, par, h)
            for n in (UNITS - 2, UNITS - 1):
                for h in range(2):
                    step(n, n % 2, h, last=(n == UNITS - 1))
            pt_high(2 * UNITS - 1)
            gate(UNITS - 1, 1, first=False)

            with act.Fori(0, KT) as f:
                act.wait_ge(conv_gated, f + 1)
                copy(c_hi[:, bass.ds(f, 1), :].rearrange("p a s -> p (a s)"), work_c[:], c_hi_ready)
            act.wait_ge(tile_done, T_CO)
            act.wait_ge(attn_stored, 2 * UNITS)
            for n in range(KT):
                copy(blocks(h_hi[:, n, :]), feature_tile(n), h_hi_ready)
            with act.Fori(0, KT) as n:
                act.wait_ge(branches_added, n + 1)
                copy(c_hi[:, bass.ds(n, 1), :].rearrange("p a s -> p (a s)"), work_c[:], c_hi_ready)
            for n in range(KT):
                act.wait_ge(psum_read, T_WO + n + 1)
                nc.scalar.activation(h_hi[:, n, :], residual(n), ACT.Copy, scale=gain[:, KT + n:KT + n + 1]
                                     ).then_inc(h_hi_ready, 1)
                if n:
                    act.wait_ge(square_added, KT + n)
                nc.scalar.activation(work_c[:], residual(n), ACT.Square).then_inc(square_ready, 1)
            rms(2)
            f_base = 0
            for c, width in enumerate(CHUNKS):
                with act.Fori(0, width) as f:
                    act.wait_ge(psum_read, f * 2 + (T_UP[c] + 1))
                    nc.scalar.activation(work_b[:, 0:S], work_a[:], ACT.Tanh, scale=0.5).then_inc(silu_tanh, 1)
                    act.wait_ge(ffn_act, f + (f_base + 1))
                    copy(c_hi[:, bass.ds(f, 1), :].rearrange("p a s -> p (a s)"), work_c[:], c_hi_ready)
                f_base += width
            for n in range(KT):
                act.wait_ge(psum_read, T_DOWN[-1] + n + 1)
                if n:
                    act.wait_ge(square_added, 2 * KT + n)
                nc.scalar.activation(work_c[:], residual(n), ACT.Square).then_inc(square_ready, 1)
                nc.scalar.activation(y[:, n, :], residual(n), ACT.Copy,
                                     scale=gain[:, 2 * KT + n:2 * KT + n + 1]).then_inc(y_scaled, 1)
            rms(3)

        @block.vector
        def _(dve):
            V = nc.vector

            def leave_psum(out, in1, t_plus_1, slot, ps=None):
                dve.wait_ge(tile_done, t_plus_1)
                V.tensor_tensor(out, (ps or slot_ps[slot])[:], in1, ALU.mult).then_inc(psum_read, 1)

            def lo_half(out, whole, hi, done):
                return V.tensor_tensor(out, whole, hi.bitcast(F32), ALU.subtract).then_inc(done, 1)

            def add_square(k, n, src):
                dve.wait_ge(square_ready, n * KT + k + 1)
                if k == 0:
                    V.tensor_copy(rstd_sq[:], src).then_inc(square_added, 1)
                else:
                    dve.wait_ge(square_added, n * KT + k)
                    V.tensor_tensor(rstd_sq[:], rstd_sq[:], src, ALU.add).then_inc(square_added, 1)

            def norm(n):
                if n > 1:
                    dve.wait_ge(ssq_split, 2 * n - 1)
                    lo_half(ssq_lo[:], rstd_sq[:], ssq_hi[:], ssq_split)
                dve.wait_ge(rms_ready, n)
                V.reciprocal(rstd[:], rstd[:]).then_inc(rstd_ready, 1)
                dve.wait_ge(rstd_ready, n)

            dve.wait_ge(setup_done, 5)
            dve.wait_ge(gains_loaded, 16)
            for k in range(KT):
                dve.wait_ge(x_loaded[k], 16)
                dve.wait_ge(h_hi_ready, k + 1)
                V.scalar_tensor_tensor(h_lo[:, k, :], residual(k), gain[:, k:k + 1],
                                       h_hi[:, k, :].bitcast(F32), ALU.mult, ALU.subtract
                                       ).then_inc(h_lo_ready, 1)
            for k in range(KT):
                add_square(k, 0, square_buf[k % 2][:, 0:S])
            dve.wait_ge(square_added, KT)
            dve.wait_ge(ssq_split, 1)
            lo_half(ssq_lo[:], rstd_sq[:], ssq_hi[:], ssq_split)
            dve.wait_ge(consts_loaded, 16 * N_CONSTS)
            V.tensor_copy(take_cur[:].rearrange("p (t k) -> p t k", t=GROUP),
                          prob[:, 0, :].unsqueeze(1).to_broadcast([P, GROUP, P])).then_inc(mask_ready, 1)
            V.tensor_copy(prev_bias[:], bias_table[:, 0:1]).then_inc(bias_set, 1)
            norm(1)
            for i in range(PAIRS):
                leave_psum(v_feature[i][:], rstd[:], T_V + i + 1, i % 2)
            V.tensor_tensor(rstd_sq[:], rstd[:], rstd[:], ALU.mult).then_inc(rstd_sq_ready, 1)

            swap = [i ^ (ROT // 2) if i < ROT else i for i in range(32)]

            def rope(i, t_plus_1, slot, dst, first=False, ps=None):
                leave_psum(work_a[:], rstd[:], t_plus_1, slot, ps)
                if not first:
                    dve.wait_ge(roped, i)
                dve.wait_ge(psum_read, t_plus_1)
                V.stream_shuffle(work_b[:, 0:S], work_a[:], swap).then_inc(swapped, 1)
                V.tensor_tensor(work_c[:], work_a[:], rope_cos[:], ALU.mult).then_inc(cos_part, 1)
                dve.wait_ge(swapped, i + 1)
                V.tensor_tensor(work_b[:, 0:S], work_b[:, 0:S], rope_sin[:], ALU.mult).then_inc(sin_part, 1)
                dve.wait_ge(cos_part, i + 1)
                dve.wait_ge(sin_part, i + 1)
                c, b = work_c[:], work_b[:, 0:S]
                if len(dst.shape) == 3:
                    c, b = blocks(c), blocks(b)
                V.tensor_tensor(dst, c, b, ALU.add).then_inc(roped, 1)

            for i in range(PAIRS):
                rope(i, T_K + i + 1, i % 2, keys[:, P + i * S:P + (i + 1) * S], first=(i == 0),
                     ps=spare_ps if i == 0 else None)

            def split_unit(n, par, first=False):
                dve.wait_ge(unit_hi, n * 3 + 1)
                lo_half(q_lo[par][:], m[:, bass.ds(n * (GROUP * P), GROUP * P)], q_hi[par][:], unit_lo)
                dve.wait_ge(unit_hi, n * 3 + 2)
                lo_half(k_lo[par][:], keys[:, bass.ds(n * P, 2 * P)], k_hi[par][:], unit_lo)
                dve.wait_ge(unit_hi, n * 3 + 3)
                lo_half(v_lo[par][:], values[:, bass.ds(n * P, 2 * P)], v_hi[par][:], unit_lo)

            for i in range(KT):
                rope(PAIRS + i, T_Q + i + 1, i % 2, feature_tile(i))
                if i == GROUP:
                    dve.wait_ge(roped, PAIRS + GROUP)
                    split_unit(0, 0, first=True)

            dve.wait_ge(mask_ready, 1)

            def begin_softmax(u):
                dve.wait_ge(prev_copied, u + 1)
                V.tensor_scalar(prev_bias[:], bias_table[:, bass.ds(u + 1, 1)], 1.0, None, ALU.mult
                                ).then_inc(bias_set, 1)
                by_head = scores_ps[:].rearrange("p (t w k) -> p t w k", t=GROUP, w=2)
                V.copy_predicated(scores[:], take_cur[:].rearrange("p (t k) -> p t k", t=GROUP),
                                  by_head[:, :, 1, :]).then_inc(scores_merged, 1)
                dve.wait_ge(scores_merged, u + 1)
                V.tensor_reduce(row_max[:], scores[:], AX.X, ALU.max).then_inc(max_ready, 1)
                dve.wait_ge(max_ready, u + 1)
                V.scalar_tensor_tensor(top[:], row_max[:], SCALE, sink[:, bass.ds(u * GROUP, GROUP)],
                                       ALU.mult, ALU.max).then_inc(top_ready, 1)
                dve.wait_ge(top_ready, u + 1)
                V.tensor_scalar(neg_max[:], top[:], -1.0, None, ALU.mult).then_inc(shift_ready, 1)
                V.tensor_tensor(sink_arg[:], sink[:, bass.ds(u * GROUP, GROUP)], top[:], ALU.subtract
                                ).then_inc(sink_arg_ready, 1)

            def end_softmax(u):
                dve.wait_ge(exp_done, u * (GROUP + 1) + (GROUP + 1))
                V.tensor_tensor(denom[:], exp_sum[:], sink_exp[:], ALU.add).then_inc(denom_ready, 1)
                dve.wait_ge(denom_ready, u + 1)
                V.reciprocal(inv_denom[:], denom[:]).then_inc(inv_ready, 1)
                dve.wait_ge(inv_ready, u + 1)
                V.tensor_tensor(prob[:], prob[:], inv_denom[:].unsqueeze(2).to_broadcast([P, GROUP, P]),
                                ALU.mult).then_inc(probs_ready, 1)

            def mask_probs(u, first=False):
                dve.wait_ge(probs_turned, u + 1)
                if not first:
                    dve.wait_ge(pt_lo_ready, u * 2)
                by_head = turn_ps.rearrange("p (t q) -> p t q", t=GROUP)
                V.tensor_tensor(pt_cur[:], by_head, keep_cur[:].unsqueeze(1).to_broadcast([P, GROUP, P]),
                                ALU.mult).then_inc(pt_masked, 1)
                dve.wait_ge(pt_masked, u * 2 + 1)
                V.tensor_tensor(pt_prev[:], by_head, pt_cur[:], ALU.subtract).then_inc(pt_masked, 1)

            def pt_low(u):
                for i, pt in enumerate((pt_cur, pt_prev)):
                    dve.wait_ge(pt_hi_ready, u * 2 + (i + 1))
                    lo_half(pt_lo[i][:], pt[:].rearrange("p t q -> p (t q)"), pt_hi[i][:], pt_lo_ready)

            def store_attention(n, h, u):
                rows = slice(h * HEAD, (h + 1) * HEAD)
                dve.wait_ge(pv_done, u + 1)
                V.tensor_scalar(m[rows, bass.ds(n * (GROUP * P), GROUP * P)], attn_ps[rows, :], 1.0, None,
                                ALU.mult).then_inc(attn_stored, 1)

            def gate(n, par, first=False):
                if not first:
                    dve.wait_ge(gate_tanh, n)
                leave_psum(work_a[:], rstd[:], n + (T_GATE + 1), par)

            def step(n, par, h, first=0, last=False):
                u = n * 2 + h
                if first != 1:
                    mask_probs(u - 1, first=(first == 2))
                begin_softmax(u)
                if first != 1:
                    pt_low(u - 1)
                if not first:
                    store_attention(n - 1, h, u - 2)
                if h == 1 and not last:
                    split_unit(n + 1, 1 - par)
                end_softmax(u)
                if h == 0 and first != 1:
                    gate(n - 1, 1 - par, first=(isinstance(n, int) and n == 1))

            for h in range(2):
                step(0, 0, h, first=h + 1)
            for h in range(2):
                step(1, 1, h)
            with by_two(dve, 2, UNITS - 2) as n:
                for par in range(2):
                    for h in range(2):
                        step(n + par, par, h)
            for n in (UNITS - 2, UNITS - 1):
                for h in range(2):
                    step(n, n % 2, h, last=(n == UNITS - 1))
            last = 2 * UNITS - 1
            mask_probs(last)
            store_attention(UNITS - 1, 0, last - 1)
            pt_low(last)
            gate(UNITS - 1, 1)
            store_attention(UNITS - 1, 1, last)

            padded = work_b
            dve.wait_ge(gate_tanh, UNITS)
            dve.wait_ge(gate_stored[0], 16 * KT)
            dve.wait_ge(gate_stored[1], 16 * KT)
            V.memset(padded[:, 0:2], 0.0).then_inc(setup_done, 1)

            def conv(f, slot):
                t = f * 3 + T_CONV

                leave_psum(work_a[:], rstd_sq[:], t + 1, slot)
                dve.wait_ge(psum_read, t + 1)
                leave_psum(padded[:, 2:S + 2], work_a[:], t + 2, 1 - slot)
                dve.wait_ge(psum_read, t + 2)
                tap = lambda j: taps[:, bass.ds(f * 3 + j, 1)]
                V.tensor_scalar(work_c[:], padded[:, 2:S + 2], tap(2), None, ALU.mult).then_inc(conv_tap, 1)
                for j in (1, 0):
                    dve.wait_ge(conv_tap, f * 3 + (2 - j))
                    V.scalar_tensor_tensor(work_c[:], padded[:, j:S + j], tap(j), work_c[:],
                                           ALU.mult, ALU.add).then_inc(conv_tap, 1)
                leave_psum(work_a[:], rstd[:], t + 3, slot)
                dve.wait_ge(psum_read, t + 3)
                dve.wait_ge(conv_tap, f * 3 + 3)
                V.tensor_tensor(work_c[:], work_c[:], work_a[:], ALU.mult).then_inc(conv_gated, 1)
                dve.wait_ge(c_hi_ready, f + 1)
                lo_half(c_lo[:, bass.ds(f, 1), :].rearrange("p a s -> p (a s)"), work_c[:],
                        c_hi[:, bass.ds(f, 1), :].rearrange("p a s -> p (a s)"), c_lo_ready)
                dve.wait_ge(c_lo_ready, f + 1)

            dve.wait_ge(setup_done, 6)
            with by_two(dve, 0, KT) as f:
                conv(f, 0)
                conv(f + 1, 1)

            for n in range(KT):
                dve.wait_ge(h_hi_ready, KT + n + 1)
                lo_half(blocks(h_lo[:, n, :]), feature_tile(n), blocks(h_hi[:, n, :]), h_lo_ready)
            for n in range(KT):
                dve.wait_ge(gate_loaded[n % 2], 16 * (n // 2 + 1))
                dve.wait_ge(tile_done, T_CO + n + 1)
                dve.wait_ge(h_lo_ready, 2 * KT)
                V.scalar_tensor_tensor(feature_tile(n), blocks(reload_buf[n % 2][:, 0:S]), 1.0,
                                       blocks(slot_ps[n % 2][:]), ALU.add, ALU.mult).then_inc(psum_read, 1)
            for n in range(KT):
                g = KT + n
                dve.wait_ge(gate_loaded[g % 2], 16 * (g // 2 + 1))
                dve.wait_ge(tile_done, T_AO + n + 1)
                dve.wait_ge(c_lo_ready, KT + n)
                V.scalar_tensor_tensor(work_c[:], reload_buf[g % 2][:, 0:S], 1.0, slot_ps[n % 2][:],
                                       ALU.add, ALU.mult).then_inc(psum_read, 1)
                dve.wait_ge(psum_read, T_AO + n + 1)
                V.tensor_tensor(blocks(work_c[:]), blocks(work_c[:]), feature_tile(n), ALU.add
                                ).then_inc(branches_added, 1)
                dve.wait_ge(c_hi_ready, KT + n + 1)
                lo_half(c_lo[:, n, :], work_c[:], c_hi[:, n, :], c_lo_ready)
            for n in range(KT):
                dve.wait_ge(x_reloaded[n % 2], 16 * (n // 2 + 1))
                dve.wait_ge(tile_done, T_WO + n + 1)
                dve.wait_ge(branches_added, KT)
                V.scalar_tensor_tensor(residual(n), slot_ps[n % 2][:], 0.5, reload_buf[n % 2][:, 0:S],
                                       ALU.mult, ALU.add).then_inc(psum_read, 1)
                dve.wait_ge(h_hi_ready, 2 * KT + n + 1)
                dve.wait_ge(psum_read, T_WO + n + 1)
                V.scalar_tensor_tensor(h_lo[:, n, :], residual(n), gain[:, KT + n:KT + n + 1],
                                       h_hi[:, n, :].bitcast(F32), ALU.mult, ALU.subtract
                                       ).then_inc(h_lo_ready, 1)
                add_square(n, 1, work_c[:])
            dve.wait_ge(square_added, 2 * KT)
            norm(2)

            f_base = 0
            for c, width in enumerate(CHUNKS):
                with dve.Fori(0, width) as f:
                    t = f * 2 + T_UP[c]
                    leave_psum(work_a[:], rstd[:], t + 1, 0)
                    dve.wait_ge(psum_read, t + 1)
                    dve.wait_ge(silu_tanh, f + (f_base + 1))
                    V.scalar_tensor_tensor(work_c[:], work_b[:, 0:S], 1.0, work_a[:], ALU.add, ALU.mult
                                           ).then_inc(silu_gate, 1)
                    dve.wait_ge(silu_gate, f + (f_base + 1))
                    leave_psum(work_a[:], rstd[:], t + 2, 1)
                    dve.wait_ge(psum_read, t + 2)
                    V.tensor_tensor(work_c[:], work_c[:], work_a[:], ALU.mult).then_inc(ffn_act, 1)
                    dve.wait_ge(ffn_act, f + (f_base + 1))
                    dve.wait_ge(c_hi_ready, f + (2 * KT + f_base + 1))
                    lo_half(c_lo[:, bass.ds(f, 1), :].rearrange("p a s -> p (a s)"), work_c[:],
                            c_hi[:, bass.ds(f, 1), :].rearrange("p a s -> p (a s)"), c_lo_ready)
                    dve.wait_ge(c_lo_ready, f + (2 * KT + f_base + 1))
                f_base += width
                final = c == len(CHUNKS) - 1
                if not final:
                    with by_two(dve, 0, KT) as n:
                        for j in range(2):
                            dve.wait_ge(tile_done, n + (T_DOWN[c] + j + 1))
                            acc = m[:, bass.ds(n * S + j * S, S)]
                            V.scalar_tensor_tensor(acc, slot_ps[j][:], 0.5, acc, ALU.mult, ALU.add
                                                   ).then_inc(psum_read, 1)
                else:
                    for n in range(KT):
                        dve.wait_ge(tile_done, T_DOWN[c] + n + 1)
                        V.scalar_tensor_tensor(residual(n), slot_ps[n % 2][:], 0.5, residual(n),
                                               ALU.mult, ALU.add).then_inc(psum_read, 1)
                        add_square(n, 2, work_c[:])
            dve.wait_ge(square_added, 3 * KT)
            norm(3)
            for n in range(KT - POOL_OUT):
                dve.wait_ge(y_scaled, n + 1)
                V.tensor_tensor(y[:, n, :], y[:, n, :], rstd[:], ALU.mult).then_inc(out_dve, 1)


def shape_constants():
    f32 = np.float32
    j = np.arange(P)
    keep_cur = (j[:, None] <= j[None, :]).astype(f32)
    take_cur = (j[None, :] <= j[:, None]).astype(f32)
    bias_table = np.zeros((P, 2 * UNITS + 1), f32)
    bias_table[:, 0:-1:2 * NB] = bias_table[:, 1:-1:2 * NB] = NEG
    inv_freq = f32(500000.0) ** (-np.arange(0, ROT, 2, dtype=f32) / f32(ROT))
    angle = np.arange(S, dtype=f32)[None, :] * inv_freq[:, None].astype(f32)
    cos, sin = np.cos(angle).astype(f32), np.sin(angle).astype(f32)
    rope_cos, rope_sin = np.ones((P, S), f32), np.zeros((P, S), f32)
    for h in range(P // HEAD):
        a, half = h * HEAD, ROT // 2
        rope_cos[a:a + half] = rope_cos[a + half:a + ROT] = cos
        rope_sin[a:a + half], rope_sin[a + half:a + ROT] = -sin, sin
    return {"ident": np.eye(P, dtype=f32), "keep_cur": keep_cur, "take_cur": take_cur, "bias_table": bias_table, "rope_cos": rope_cos, "rope_sin": rope_sin}


def pack_weights(w_in, w_conv_out, w_attn_out, w_o, w_gate_up, w_down):
    def cols(w, first, n):
        v = w[:, first:first + n * P].reshape(-1, P, n, P)
        return v.transpose(2, 1, 0, 3)

    bounds = np.cumsum([0, D, D, D, D, N_KV * HEAD, N_KV * HEAD, D, D])
    cb, cc, cx, q, k, v, gate_c, gate_a = bounds[:-1]
    head_order = np.array([2 * GROUP * p + GROUP * e + t for p in range(PAIRS) for t in range(GROUP)
                           for e in range(2)])
    features = (head_order[:, None] * HEAD + np.arange(HEAD)[None, :]).ravel()
    conv = np.stack([cols(w_in, c, KT) for c in (cc, cx, cb)], 1).reshape(3 * KT, P, KT, P)
    parts = [cols(w_in, v, PAIRS), cols(w_in, k, PAIRS), cols(w_in[:, q:q + D][:, features], 0, KT),
             cols(w_in, gate_c, KT), cols(w_in, gate_a, KT), conv,
             cols(w_conv_out, 0, KT), cols(w_attn_out[features], 0, KT), cols(w_o, 0, KT)]
    f0 = 0
    for width in CHUNKS:
        gu = np.stack([cols(w_gate_up, f0 * P, width), cols(w_gate_up, D_FF + f0 * P, width)], 1)
        parts.append(gu.reshape(2 * width, P, KT, P))
        down = np.zeros((KT, P, KT, P), w_down.dtype)
        down[:, :, :width] = cols(w_down[f0 * P:(f0 + width) * P], 0, KT)
        parts.append(down)
        f0 += width
    return np.ascontiguousarray(np.concatenate(parts, 0).reshape(TILES, P, KT * P))


def kernel(x, g_mix, w_in, conv_w, attn_sinks, w_conv_out, w_attn_out, w_o, g_ffn, w_gate_up,
           w_down, g_final):
    import concourse.bacc as bacc
    from concourse.bass_utils import run_bass_kernel_spmd

    arr = np.asarray
    by_tile = lambda v: arr(v).reshape(-1, KT, P).transpose(2, 0, 1)
    s = arr(attn_sinks)[0].reshape(PAIRS, 1, 2, GROUP)
    s = np.broadcast_to(s, (PAIRS, NB, 2, GROUP)).reshape(1, -1)
    arrays = {
        "x_t": np.ascontiguousarray(arr(x)[0].T).reshape(KT, P, S),
        "w_stream": pack_weights(*(arr(w)[0] for w in (w_in, w_conv_out, w_attn_out, w_o, w_gate_up, w_down))),
        "gains": np.ascontiguousarray(np.concatenate(
            [by_tile(arr(g_mix)[0]), by_tile(arr(g_ffn)[0]), by_tile(arr(g_final))], 1).reshape(P, 3 * KT)),
        "conv_w": np.ascontiguousarray(by_tile(arr(conv_w)[0]).transpose(0, 2, 1).reshape(P, 3 * KT)),
        "sinks": np.ascontiguousarray(np.broadcast_to(s, (P, s.shape[1]))),
    }
    consts = shape_constants()
    nc = bacc.Bacc("TRN2", target_bir_lowering=False, num_devices=1)

    def dram(name, a):
        return nc.dram_tensor(name, a.shape, mybir.dt.from_np(a.dtype), kind="ExternalInput").ap()

    aps = {name: dram(name, a) for name, a in arrays.items()}
    const_aps = {name: dram("const_" + name, a) for name, a in consts.items()}
    out_t = nc.dram_tensor("out_t", (KT, P, S), F32, kind="ExternalOutput").ap()
    scratch = nc.dram_tensor("gate_scratch", (2 * KT, P, S), F32, kind="Internal").ap()
    block_kernel(nc, *(aps[n] for n in ("x_t", "w_stream", "gains", "conv_w", "sinks")), out_t,
                 const_aps, scratch)
    arrays.update({"const_" + name: a for name, a in consts.items()})
    r = run_bass_kernel_spmd(nc, [arrays], core_ids=[0])
    got = r.results[0]["out_t"]
    return np.ascontiguousarray(got.reshape(D, S).T).reshape(1, S, D)
```

```python
from contextlib import ExitStack, contextmanager

import numpy as np

import concourse.bass as bass
from concourse import mybir

F32 = mybir.dt.float32
F32R = mybir.dt.float32r
U8 = mybir.dt.uint8
ALU = mybir.AluOpType
ACT = mybir.ActivationFunctionType
AX = mybir.AxisListType

P = 128
D = 1024
S = 1024
KT = D // P
HALF = 512
HEAD = 64
N_HEADS = 16
N_KV = 4
GROUP = N_HEADS // N_KV
PAIRS = N_KV // 2
NB = S // P
UNITS = PAIRS * NB
D_FF = ((8 * D // 3 + 255) // 256) * 256
FT = D_FF // P
CHUNKS = (8, 8, 6)
ROT = HEAD // 4
SCALE = float(HEAD) ** -0.5
EPS = 1e-5
NEG = -1e30

T_V = 0
T_K = T_V + PAIRS
T_Q = T_K + PAIRS
T_GATE = T_Q + KT
T_CONV = T_GATE + 2 * KT
T_CO = T_CONV + 3 * KT
T_AO = T_CO + KT
T_WO = T_AO + KT
T_UP = []
T_DOWN = []
_t = T_WO + KT
for _f in CHUNKS:
    T_UP.append(_t)
    T_DOWN.append(_t + 2 * _f)
    _t += 2 * _f + KT
TILES = _t
assert sum(CHUNKS) == FT and TILES % 2 == 0


PIECES = ((0, 512), (512, 768), (768, 1024))
RECIP = 256

X_LOADS = ((0, 1), (1, 2), (2, 4), (4, 6), (6, 8))


def x_load_of(k):
    return next(i for i, (a, b) in enumerate(X_LOADS) if a <= k < b)


@contextmanager
def by_two(engine, first, last):
    with engine.Fori(0, (last - first) // 2) as i:
        yield i * 2 + first


def block_kernel(nc, x_t, w_stream, gains, conv_w, sinks, out_t, consts, gate_scratch):
    with ExitStack() as ctx:
        def sb(name, shape, dt=F32):
            return ctx.enter_context(nc.sbuf_tensor(name, shape, dt))

        def sem(name):
            return ctx.enter_context(nc.semaphore(name))

        def psum(name, shape):
            return ctx.enter_context(nc.psum_tensor(name, shape, F32))

        w_raw = [sb(f"w_raw{i}", [P, KT * P]) for i in range(2)]
        w_hi = [sb(f"w_hi{i}", [P, KT * P], F32R) for i in range(2)]
        w_lo = [sb(f"w_lo{i}", [P, KT * P], F32R) for i in range(2)]
        h_at = nc.sbuf_base
        h_hi = sb("h_hi", [P, KT, S], F32R)
        h_lo = sb("h_lo", [P, KT, S], F32R)
        m = sb("m", [P, KT * S])
        rstd = sb("rstd", [P, S])
        rstd_sq = sb("rstd_sq", [P, S])
        work_a = sb("work_a", [P, S])
        work_b_at = nc.sbuf_base
        work_b = sb("work_b", [P, S + 8])
        work_c_at = nc.sbuf_base
        work_c = sb("work_c", [P, S])
        ident = sb("ident", [P, P])
        mean_w = sb("mean_w", [P, P], F32R)
        keep_cur = sb("keep_cur", [P, P])
        take_cur = sb("take_cur", [P, GROUP * P], U8)
        bias_table = sb("bias_table", [P, 2 * UNITS + 1])
        prev_bias = sb("prev_bias", [P, 1])
        zero = sb("zero", [P, 1])
        gain = sb("gain", [P, 3 * KT])
        taps = sb("taps", [P, 3 * KT])
        sink = sb("sink", [P, 2 * UNITS * GROUP])
        eps = sb("eps", [P, 1])
        row_max = sb("row_max", [P, GROUP])
        top = sb("top", [P, GROUP])
        neg_max = sb("neg_max", [P, GROUP])
        sink_arg = sb("sink_arg", [P, GROUP])
        sink_exp = sb("sink_exp", [P, GROUP])
        exp_sum = sb("exp_sum", [P, GROUP])
        denom = sb("denom", [P, GROUP])
        inv_denom = sb("inv_denom", [P, GROUP])

        with ExitStack() as attention_only:
            def asb(name, shape, dt=F32):
                return attention_only.enter_context(nc.sbuf_tensor(name, shape, dt))

            rope_cos = asb("rope_cos", [P, S])
            rope_sin = asb("rope_sin", [P, S])
            keys = asb("keys", [P, (UNITS + 1) * P])
            values = asb("values", [P, (UNITS + 1) * P])
            with ExitStack() as before_attention:
                v_feature = [before_attention.enter_context(nc.sbuf_tensor(f"v_feature{i}", [P, S], F32))
                             for i in range(PAIRS)]
            q_hi = [asb(f"q_hi{i}", [P, GROUP * P], F32R) for i in range(2)]
            q_lo = [asb(f"q_lo{i}", [P, GROUP * P], F32R) for i in range(2)]
            k_hi = [asb(f"k_hi{i}", [P, 2 * P], F32R) for i in range(2)]
            k_lo = [asb(f"k_lo{i}", [P, 2 * P], F32R) for i in range(2)]
            v_both = [asb(f"v_both{i}", [P, 2, 2, 2, HEAD], F32R) for i in range(2)]
            scores = asb("scores", [P, GROUP, P])
            of_lo = asb("of_lo", [P, GROUP * P])
            prob = asb("prob", [P, GROUP, P])
            pt_cur = asb("pt_cur", [P, GROUP, P])
            pt_prev = asb("pt_prev", [P, GROUP, P])
            pt_hi = [asb(f"pt_hi{i}", [P, GROUP * P], F32R) for i in range(2)]
            pt_lo = [asb(f"pt_lo{i}", [P, GROUP * P], F32R) for i in range(2)]
        c_hi = sb("c_hi", [P, KT, S], F32R)
        c_lo = sb("c_lo", [P, KT, S], F32R)
        ssq_hi = nc.alloc_sbuf_tensor_at("ssq_hi", [P, S], F32R, offset=work_b_at)
        ssq_lo = nc.alloc_sbuf_tensor_at("ssq_lo", [P, S], F32R, offset=work_c_at)
        WD_COLS = CHUNKS[-1] * P
        wd_hi = nc.alloc_sbuf_tensor_at("wd_hi", [P, KT - 2, WD_COLS], F32R, offset=h_at)
        wd_lo = nc.alloc_sbuf_tensor_at("wd_lo", [P, KT - 2, WD_COLS], F32R, offset=h_at + KT * S * 4)

        slot_ps = [psum(f"slot_ps{i}", [P, S]) for i in range(2)]
        scores_ps = psum("scores_ps", [P, S])
        spare_ps = psum("spare_ps", [P, S])
        turn_ps = spare_ps[:, 0:GROUP * P]
        attn_ps = spare_ps[:, GROUP * P:2 * GROUP * P]

        def feature_tile(kt):
            pair, head = kt // GROUP, kt % GROUP
            v = m[:].rearrange("p (a b t q) -> p a b t q", a=PAIRS, b=NB, t=GROUP)
            return v[:, pair, :, head, :]

        def blocks(ap):
            return ap.rearrange("p (b q) -> p b q", b=NB)

        def residual(n):
            return m[:, n * S:(n + 1) * S]

        gains_loaded = sem("gains_loaded")
        consts_loaded = sem("consts_loaded")
        x_loaded = [sem(f"x_loaded{i}") for i in range(len(X_LOADS))]
        raw_loaded = [sem(f"raw_loaded{i}") for i in range(2)]
        table_loaded = sem("table_loaded")
        first_hi = sem("first_hi")
        first_split = sem("first_split")
        raw_hi = sem("raw_hi")
        weights_split = sem("weights_split")
        setup_done = sem("setup_done")
        tile_done = sem("tile_done")
        psum_read = sem("psum_read")
        h_hi_ready = sem("h_hi_ready")
        h_lo_ready = sem("h_lo_ready")
        c_hi_ready = sem("c_hi_ready")
        c_lo_ready = sem("c_lo_ready")
        square_ready = sem("square_ready")
        square_added = sem("square_added")
        ssq_split = sem("ssq_split")
        mean_done = sem("mean_done")
        rms_ready = sem("rms_ready")
        rstd_ready = sem("rstd_ready")
        rstd_sq_ready = sem("rstd_sq_ready")
        swapped = sem("swapped")
        cos_part = sem("cos_part")
        sin_part = sem("sin_part")
        roped = sem("roped")
        v_turned = sem("v_turned")
        v_stored = sem("v_stored")
        unit_hi = sem("unit_hi")
        unit_lo = sem("unit_lo")
        scores_done = sem("scores_done")
        mask_ready = sem("mask_ready")
        bias_set = sem("bias_set")
        prev_copied = sem("prev_copied")
        scores_merged = sem("scores_merged")
        max_ready = sem("max_ready")
        top_ready = sem("top_ready")
        shift_ready = sem("shift_ready")
        sink_arg_ready = sem("sink_arg_ready")
        exp_done = sem("exp_done")
        denom_ready = sem("denom_ready")
        inv_ready = sem("inv_ready")
        probs_ready = sem("probs_ready")
        probs_turned = sem("probs_turned")
        pt_masked = sem("pt_masked")
        pt_hi_ready = sem("pt_hi_ready")
        pt_lo_ready = sem("pt_lo_ready")
        pv_done = sem("pv_done")
        lo_moved = sem("lo_moved")
        attn_stored = sem("attn_stored")
        gate_tanh = sem("gate_tanh")
        gate_stored = [sem(f"gate_stored{i}") for i in range(2)]
        gate_loaded = [sem(f"gate_loaded{i}") for i in range(2)]
        conv_tap = sem("conv_tap")
        conv_gated = sem("conv_gated")
        branches_added = sem("branches_added")
        x_reloaded = [sem(f"x_reloaded{i}") for i in range(2)]
        silu_tanh = sem("silu_tanh")
        silu_gate = sem("silu_gate")
        ffn_act = sem("ffn_act")
        y_scaled = sem("y_scaled")
        out_dve = sem("out_dve")
        out_pool = sem("out_pool")
        out_stored = sem("out_stored")

        N_CONSTS = len(consts) + 2
        FIRST_PARTS = 4
        POOL_OUT = 3
        LAST_PIECE = len(PIECES) - 1

        def scaled_by_pool(p, n):
            return p < LAST_PIECE or n >= KT - POOL_OUT

        def pool_scaled_before(p, n):
            return p * KT + (n if p < LAST_PIECE else n - (KT - POOL_OUT))

        def rstd_count(p):
            return 2 + PIECES[p][1] // RECIP

        gate_buf = [work_b, work_c]
        square_buf = [work_a, work_b]
        reload_buf = [work_a, work_b]

        def final_square(i, width):
            return work_a[:, i % 2 * HALF:i % 2 * HALF + width]

        block = ctx.enter_context(nc.Block())

        @block.sync
        def _(sp):
            def load_weights(t_expr, slot, count, first=False):
                if not first:
                    sp.wait_ge(weights_split, count - 1)
                sp.dma_start(w_raw[slot][:], w_stream[bass.ds(t_expr, 1), :, :].rearrange("a p n -> (a p) n")
                             ).then_inc(raw_loaded[slot], 16)

            sp.dma_start(gain[:], gains).then_inc(gains_loaded, 16)
            sp.dma_start(residual(0), x_t[0]).then_inc(x_loaded[0], 16)
            load_weights(0, 0, 0, first=True)
            for i, (a, b) in enumerate(X_LOADS[1:]):
                sp.dma_start(m[:, a * S:b * S].rearrange("p (k s) -> p k s", s=S),
                             x_t[a:b].rearrange("k p s -> p k s")).then_inc(x_loaded[i + 1], 16)
            load_weights(1, 1, 0, first=True)
            sp.wait_ge(x_loaded[-1], 16)
            for dst, src in ((taps, conv_w), (sink, sinks), (ident, consts["ident"]),
                             (keep_cur, consts["keep_cur"]),
                             (prob[:, 0, :], consts["take_cur"]), (bias_table, consts["bias_table"]),
                             (rope_cos, consts["rope_cos"]), (rope_sin, consts["rope_sin"])):
                sp.dma_start(dst[:], src).then_inc(consts_loaded, 16)
            sp.wait_ge(first_split, FIRST_PARTS)
            load_weights(2, 0, 0, first=True)
            load_weights(3, 1, 2)
            with by_two(sp, 4, T_GATE + 4) as t:
                for j in range(2):
                    load_weights(t + j, j, t + (j - 1))
            with by_two(sp, T_GATE + 4, T_CONV + 4) as t:
                for j in range(2):
                    load_weights(t + j, j, t + (j - 1))
                    sp.wait_ge(gate_tanh, t + (j - (T_GATE + 3)))
                    sp.dma_start(gate_scratch[bass.ds(t + (j - (T_GATE + 4)), 1), :, :].rearrange("a p n -> (a p) n"),
                                 gate_buf[j][:, 0:S]).then_inc(gate_stored[j], 16)
            with by_two(sp, T_CONV + 4, T_CO + 2) as t:
                for j in range(2):
                    load_weights(t + j, j, t + (j - 1))
            for i in range(2):
                sp.wait_ge(gate_stored[i], 16 * KT)
            sp.wait_ge(conv_gated, KT)
            sp.wait_ge(conv_tap, 3 * KT)

            def reload(j, t, n, source, done):
                sp.wait_ge(psum_read, t - 1)
                sp.dma_start(reload_buf[j][:, 0:S], source[bass.ds(n, 1), :, :].rearrange("a p n -> (a p) n")
                             ).then_inc(done[j], 16)
                load_weights(t + 2, j, t + 1)

            with by_two(sp, 0, 2 * KT) as n:
                for j in range(2):
                    reload(j, n + (T_CO + j), n + j, gate_scratch, gate_loaded)
            with by_two(sp, 0, KT) as n:
                for j in range(2):
                    reload(j, n + (T_WO + j), n + j, x_t, x_reloaded)
            with by_two(sp, T_UP[0] + 2, TILES) as t:
                for j in range(2):
                    load_weights(t + j, j, t + (j - 1))
            for p, (a, b) in enumerate(PIECES):
                for n in range(KT):
                    if scaled_by_pool(p, n):
                        sp.wait_ge(out_pool, pool_scaled_before(p, n) + 1)
                    else:
                        sp.wait_ge(out_dve, n + 1)
                    sp.dma_start(out_t[n][:, a:b], residual(n)[:, a:b]).then_inc(out_stored, 16)
            sp.wait_ge(out_stored, 16 * KT * len(PIECES))

        @block.gpsimd
        def _(pool):
            pool.memset(zero[:], 0.0).then_inc(setup_done, 1)
            pool.memset(mean_w[:].bitcast(F32), 1.0 / D).then_inc(setup_done, 1)
            pool.memset(eps[:], EPS).then_inc(setup_done, 1)
            pool.memset(keys[:, 0:P], 0.0).then_inc(setup_done, 1)
            pool.memset(values[:, 0:P], 0.0).then_inc(setup_done, 1)

            def split(slot, loads, t_plus_1, first):
                pool.wait_ge(raw_loaded[slot], loads)
                if not first:
                    pool.wait_ge(tile_done, t_plus_1 - 2)
                nc.gpsimd.tensor_tensor(w_hi[slot][:], w_raw[slot][:], zero[:].to_broadcast([P, KT * P]),
                                        ALU.add).then_inc(raw_hi, 1)
                pool.wait_ge(raw_hi, t_plus_1 - 1)
                nc.gpsimd.tensor_tensor(w_lo[slot][:], w_raw[slot][:], w_hi[slot][:].bitcast(F32),
                                        ALU.subtract).then_inc(weights_split, 1)

            pool.wait_ge(setup_done, 1)
            pool.wait_ge(raw_loaded[0], 16)
            cols = KT * P // FIRST_PARTS
            for i in range(FIRST_PARTS):
                part = slice(i * cols, (i + 1) * cols)
                nc.gpsimd.tensor_tensor(w_hi[0][:, part], w_raw[0][:, part], zero[:].to_broadcast([P, cols]),
                                        ALU.add).then_inc(first_hi, 1)
                pool.wait_ge(first_hi, i + 1)
                nc.gpsimd.tensor_tensor(w_lo[0][:, part], w_raw[0][:, part], w_hi[0][:, part].bitcast(F32),
                                        ALU.subtract).then_inc(first_split, 1)
            split(1, 16, 2, True)
            with pool.Fori(1, T_GATE // 2) as i:
                for j in range(2):
                    split(j, i * 16 + 16, i * 2 + (j + 1), False)

            def split_unit(n, par):
                v = values[:, bass.ds(n * P, 2 * P)].rearrange("p (x d) -> p x d", d=HEAD)
                v_by_head = [v_both[par][:, :, :, i, :].rearrange("p b h d -> p (b h) d") for i in range(2)]
                for i, (lo, whole, hi) in enumerate((
                        (q_lo[par][:], m[:, bass.ds(n * (GROUP * P), GROUP * P)], q_hi[par][:]),
                        (k_lo[par][:], keys[:, bass.ds(n * P, 2 * P)], k_hi[par][:]),
                        (v_by_head[1], v, v_by_head[0]))):
                    pool.wait_ge(unit_hi, n * 3 + (i + 1))
                    nc.gpsimd.tensor_tensor(lo, whole, hi.bitcast(F32), ALU.subtract).then_inc(unit_lo, 1)

            split(0, 8 * T_GATE + 16, T_GATE + 1, False)
            split_unit(0, 0)
            with by_two(pool, 0, UNITS - 2) as n:
                for j in range(2):
                    split(1 - j, n * 8 + (8 * T_GATE + 16 * (j + 1)), n + (T_GATE + j + 2), False)
                    split_unit(n + (j + 1), 1 - j)
            split(1, 8 * (T_CONV - 2) + 16, T_CONV, False)
            split_unit(UNITS - 1, 1)
            with pool.Fori(T_CONV // 2, T_DOWN[-1] // 2 + 1) as i:
                for j in range(2):
                    split(j, i * 16 + 16, i * 2 + (j + 1), False)
            pool.wait_ge(tile_done, T_DOWN[-1])
            for n in range(2, KT):
                t = T_DOWN[-1] + n
                hi, lo, raw = wd_hi[:, n - 2, :], wd_lo[:, n - 2, :], w_raw[t % 2][:, 0:WD_COLS]
                pool.wait_ge(raw_loaded[t % 2], 16 * (t // 2 + 1))
                nc.gpsimd.tensor_tensor(hi, raw, zero[:].to_broadcast([P, WD_COLS]), ALU.add).then_inc(raw_hi, 1)
                pool.wait_ge(raw_hi, t)
                nc.gpsimd.tensor_tensor(lo, raw, hi.bitcast(F32), ALU.subtract).then_inc(weights_split, 1)
            for p, (a, b) in enumerate(PIECES):
                pool.wait_ge(rstd_ready, rstd_count(p))
                for n in range(KT):
                    if scaled_by_pool(p, n):
                        pool.wait_ge(y_scaled, p * KT + n + 1)
                        y = residual(n)[:, a:b]
                        nc.gpsimd.tensor_tensor(y, y, rstd[:, a:b], ALU.mult).then_inc(out_pool, 1)

        @block.tensor
        def _(pe):
            def product(slot, rhs_hi, rhs_lo, k_tiles=KT, halves=(0, 1), ready=None, between=None,
                        ps=None, parts=None):
                ps = slot_ps[slot] if ps is None else ps
                last = None
                for k in range(k_tiles):
                    if parts is not None and k % parts[1] == 0:
                        pe.wait_ge(parts[0], k // parts[1] + 1)
                    for i, (w, r) in enumerate(((w_hi, rhs_hi), (w_hi, rhs_lo), (w_lo, rhs_hi))):
                        if ready is not None and i < 2:
                            pe.wait_ge(ready[i], ready[2] + k + 1)
                        for s in halves:
                            cols = slice(s * HALF, (s + 1) * HALF)
                            last = nc.tensor.matmul(ps[:, cols], w[slot][:, k * P:(k + 1) * P],
                                                    r[:, k, cols], start=(k == 0 and i == 0),
                                                    stop=(k == k_tiles - 1 and i == 2))
                    if between is not None and between[0] == k:
                        between[1]()
                return last

            def slot_free(t_minus_1):
                pe.wait_ge(psum_read, t_minus_1)

            def tile(t, slot, rhs, **how):
                if not isinstance(t, int) or t > 0:
                    pe.wait_ge(weights_split, t)
                if not isinstance(t, int) or t >= 3:
                    slot_free(t + (-1))
                product(slot, *rhs, **how).then_inc(tile_done, 1)

            def tiles(first, last, rhs, k_tiles=KT, ready=None):
                with by_two(pe, first, last) as t:
                    tile(t, 0, rhs, k_tiles=k_tiles, ready=ready)
                    tile(t + 1, 1, rhs, k_tiles=k_tiles)

            def mean_square(n, pieces=((0, HALF), (HALF, S))):
                pe.wait_ge(ssq_split, 2 * n)
                for a, b in pieces:
                    cols = slice(a, b)
                    nc.tensor.matmul(scores_ps[:, cols], mean_w[:], ssq_hi[:, cols], start=True, stop=False)
                    last = nc.tensor.matmul(scores_ps[:, cols], mean_w[:], ssq_lo[:, cols],
                                            start=False, stop=True)
                last.then_inc(mean_done, 1)

            def turn_values(i):
                pe.wait_ge(psum_read, T_V + i + 1)
                if i:
                    pe.wait_ge(v_stored, i)
                else:
                    pe.wait_ge(rms_ready, 1)
                for b in range(NB):
                    last = nc.tensor.transpose(scores_ps[:, b * P:(b + 1) * P],
                                               v_feature[i][:, b * P:(b + 1) * P], ident[:])
                last.then_inc(v_turned, 1)

            H = (h_hi, h_lo)
            C = (c_hi, c_lo)
            tile(0, 0, H, ready=(h_hi_ready, h_lo_ready, 0), parts=(first_split, KT // FIRST_PARTS))
            tile(1, 1, H, between=(6, lambda: mean_square(1)))
            tile(2, 0, H, ps=spare_ps)
            tile(3, 1, H)
            pe.wait_ge(consts_loaded, 16 * N_CONSTS)
            tile(4, 0, H, between=(4, lambda: turn_values(0)))
            tile(5, 1, H, between=(4, lambda: turn_values(1)))
            tiles(6, T_GATE, H)

            def score(n, par, h):
                u = n * 2 + h
                if h == 0:
                    pe.wait_ge(unit_hi, n * 3 + 2)
                    pe.wait_ge(unit_lo, n * 3 + 2)
                if not isinstance(u, int) or u > 0:
                    pe.wait_ge(scores_merged, u)
                rows = slice(h * HEAD, (h + 1) * HEAD)
                for t in range(GROUP):
                    dst = scores_ps[:, t * 2 * P:(t + 1) * 2 * P]
                    q_cols = slice(t * P, (t + 1) * P)
                    for i, (q, k) in enumerate(((q_hi, k_hi), (q_lo, k_hi), (q_hi, k_lo))):
                        last = nc.tensor.matmul(dst, q[par][rows, q_cols], k[par][rows, :],
                                                start=(i == 0), stop=(i == 2))
                last.then_inc(scores_done, 1)

            def turn_probs(u):
                pe.wait_ge(probs_ready, u + 1)
                if not isinstance(u, int) or u > 0:
                    pe.wait_ge(pt_masked, u * 2)
                for t in range(GROUP):
                    last = nc.tensor.transpose(turn_ps[:, t * P:(t + 1) * P], prob[:, t, :], ident[:])
                last.then_inc(probs_turned, 1)

            def weigh_values(par, h, u):
                pe.wait_ge(pt_hi_ready, u * 2 + 2)
                pe.wait_ge(pt_lo_ready, u * 2 + 2)
                if not isinstance(u, int) or u > 0:
                    pe.wait_ge(attn_stored, u)
                n = 0
                for pt_of, v_block in ((0, 1), (1, 0)):
                    v = v_both[par][:, v_block, h].rearrange("p a d -> p (a d)")
                    for p in (pt_hi, pt_lo):
                        last = nc.tensor.matmul(attn_ps, v, p[pt_of][:], start=(n == 0), stop=(n == 3))
                        n += 1
                last.then_inc(pv_done, 1)

            def attention_step(n, par, h, first_unit=False):
                u = n * 2 + h
                score(n, par, h)
                if not first_unit:
                    if h == 0:
                        pe.wait_ge(unit_hi, n * 3)
                        pe.wait_ge(unit_lo, n * 3)
                    weigh_values(1 - par, h, u - 2)
                if not (first_unit and h == 0):
                    turn_probs(u - 1)
                if h == 0:
                    pe.wait_ge(weights_split, n + T_GATE)
                    slot_free(n + (T_GATE - 1))
                done = product(par, *H, halves=(h,))
                if h == 1:
                    done.then_inc(tile_done, 1)

            for n in range(2):
                for h in range(2):
                    attention_step(n, n, h, first_unit=(n == 0))
            with by_two(pe, 2, UNITS) as n:
                for par in range(2):
                    for h in range(2):
                        attention_step(n + par, par, h)
            pe.wait_ge(unit_hi, 3 * UNITS)
            pe.wait_ge(unit_lo, 3 * UNITS)
            weigh_values(1, 0, 2 * UNITS - 2)
            turn_probs(2 * UNITS - 1)
            tile(T_CONV, 0, H)
            weigh_values(1, 1, 2 * UNITS - 1)
            tile(T_CONV + 1, 1, H)
            tiles(T_CONV + 2, T_CO, H)
            tiles(T_CO, T_AO, C, ready=(c_hi_ready, c_lo_ready, 0))
            tiles(T_AO, T_WO, H, ready=(h_hi_ready, h_lo_ready, KT))
            tiles(T_WO, T_UP[0], C, ready=(c_hi_ready, c_lo_ready, KT))
            c_base = 2 * KT
            for c, width in enumerate(CHUNKS):
                if c == 0:
                    tile(T_UP[0], 0, H, ready=(h_hi_ready, h_lo_ready, 2 * KT))
                    tile(T_UP[0] + 1, 1, H, between=(1, lambda: mean_square(2)))
                    tiles(T_UP[0] + 2, T_DOWN[0], H)
                else:
                    tiles(T_UP[c], T_DOWN[c], H)
                if c < len(CHUNKS) - 1:
                    tiles(T_DOWN[c], T_DOWN[c] + KT, C, k_tiles=width, ready=(c_hi_ready, c_lo_ready, c_base))
                    c_base += width

            def down(i, k_tiles):
                (a, b), n = PIECES[i // KT], i % KT
                hi, lo = (w_hi[n], w_lo[n]) if n < 2 else (wd_hi[:, n - 2, :], wd_lo[:, n - 2, :])
                for k in k_tiles:
                    rows = slice(k * P, (k + 1) * P)
                    for j, (w, c) in enumerate(((hi, c_hi), (hi, c_lo), (lo, c_hi))):
                        last = nc.tensor.matmul(slot_ps[i % 2][:, a:b], w[:, rows], c[:, k, a:b],
                                                start=(k == 0 and j == 0), stop=(k == width - 1 and j == 2))
                return last

            for i in range(2):
                pe.wait_ge(weights_split, T_DOWN[-1] + i)
                slot_free(T_DOWN[-1] + i - 1)
                if i == 0:
                    pe.wait_ge(c_hi_ready, c_base + width - 1)
                    pe.wait_ge(c_lo_ready, c_base + width - 1)
                down(i, range(width - 1))
            pe.wait_ge(c_hi_ready, c_base + width)
            pe.wait_ge(c_lo_ready, c_base + width)
            for i in range(2):
                down(i, (width - 1,)).then_inc(tile_done, 1)
            for i in range(2, KT * len(PIECES)):
                if i < KT:
                    pe.wait_ge(weights_split, T_DOWN[-1] + i)
                slot_free(T_DOWN[-1] + i - 1)
                down(i, range(width)).then_inc(tile_done, 1)
                p, n = i // KT, i % KT
                if p > 0 and n == 1:
                    mean_square(2 + p, (PIECES[p - 1],))
            mean_square(3 + LAST_PIECE, (PIECES[-1],))

        @block.scalar
        def _(act):

            def copy(dst, src, done):
                return nc.scalar.activation(dst, src, ACT.Copy).then_inc(done, 1)

            act.wait_ge(setup_done, 5)
            copy(inv_denom[:, 0:1], zero[:], table_loaded)
            act.wait_ge(gains_loaded, 16)
            for k in range(KT):
                act.wait_ge(x_loaded[x_load_of(k)], 16)
                nc.scalar.activation(h_hi[:, k, :], residual(k), ACT.Copy, scale=gain[:, k:k + 1]
                                     ).then_inc(h_hi_ready, 1)

            def rms(n):
                act.wait_ge(square_added, n * KT)
                copy(ssq_hi[:], rstd_sq[:], ssq_split)
                act.wait_ge(mean_done, n)
                nc.scalar.activation(rstd[:], scores_ps[:], ACT.Sqrt, bias=eps[:]).then_inc(rms_ready, 1)

            for k in range(KT):
                if k >= 2:
                    act.wait_ge(square_added, k - 1)
                nc.scalar.activation(square_buf[k % 2][:, 0:S], residual(k), ACT.Square
                                     ).then_inc(square_ready, 1)
            rms(1)
            for i in range(PAIRS):
                act.wait_ge(v_turned, i + 1)
                copy(values[:, P + i * S:P + (i + 1) * S], scores_ps[:], v_stored)

            def split_qk(n, par):
                copy(q_hi[par][:], m[:, bass.ds(n * (GROUP * P), GROUP * P)], unit_hi)
                copy(k_hi[par][:], keys[:, bass.ds(n * P, 2 * P)], unit_hi)

            def split_v(n, par, first=False):
                if not first:
                    act.wait_ge(pv_done, n * 2 + (-2))
                copy(v_both[par][:, :, :, 0, :].rearrange("p b h d -> p (b h) d"),
                     values[:, bass.ds(n * P, 2 * P)].rearrange("p (x d) -> p x d", d=HEAD), unit_hi)

            act.wait_ge(mask_ready, 1)

            def softmax(u, before_exp=None):
                act.wait_ge(scores_done, u + 1)
                if not isinstance(u, int) or u > 0:
                    act.wait_ge(exp_done, u * (GROUP + 1))
                act.wait_ge(bias_set, u + 1)
                by_head = scores_ps[:].rearrange("p (t w k) -> p t w k", t=GROUP, w=2)
                nc.scalar.activation(scores[:], by_head[:, :, 0, :], ACT.Identity,
                                     bias=prev_bias[:]).then_inc(prev_copied, 1)
                if before_exp is not None:
                    before_exp()
                act.wait_ge(shift_ready, u + 1)
                if not isinstance(u, int) or u > 0:
                    act.wait_ge(probs_turned, u)
                    act.wait_ge(denom_ready, u)
                for t in range(GROUP):
                    nc.scalar.activation(prob[:, t, :], scores[:, t, :], ACT.Exp, bias=neg_max[:, t:t + 1],
                                         scale=SCALE, accum_out=exp_sum[:, t:t + 1]).then_inc(exp_done, 1)
                act.wait_ge(sink_arg_ready, u + 1)
                nc.scalar.activation(sink_exp[:], sink_arg[:], ACT.Exp).then_inc(exp_done, 1)

            def move_lo(u):
                act.wait_ge(pv_done, u + 1)
                if not isinstance(u, int) or u > 0:
                    act.wait_ge(attn_stored, u)
                copy(of_lo[0:HEAD, :], attn_ps[HEAD:2 * HEAD, :], lo_moved)

            def pt_high(u):
                if not isinstance(u, int) or u > 0:
                    act.wait_ge(pv_done, u)
                for i, pt in enumerate((pt_cur, pt_prev)):
                    act.wait_ge(pt_masked, u * 2 + (i + 1))
                    copy(pt_hi[i][:], pt[:].rearrange("p t q -> p (t q)"), pt_hi_ready)

            def gate(n, par, first):
                act.wait_ge(psum_read, n + (T_GATE + 1))
                if not first:
                    act.wait_ge(gate_stored[par], n * 8 + (-8 * par))
                nc.scalar.activation(gate_buf[par][:, 0:S], work_a[:], ACT.Tanh, scale=0.5
                                     ).then_inc(gate_tanh, 1)

            def step(n, par, h, first=False, second=False, last=False):
                u = n * 2 + h

                def for_others():
                    if not (isinstance(n, int) and n == 0):
                        move_lo(u - 2)
                    if h == 0 and not last:
                        split_qk(n + 1, 1 - par)
                    if h == 1 and not last:
                        split_v(n + 1, 1 - par, first=(isinstance(n, int) and n == 0))
                    if h == 1 and not (isinstance(n, int) and n == 0):
                        gate(n - 1, 1 - par, first=second)

                softmax(u, before_exp=for_others)
                if not first:
                    pt_high(u - 1)

            act.wait_ge(roped, PAIRS + GROUP)
            act.wait_ge(v_stored, PAIRS)
            split_qk(0, 0)
            split_v(0, 0, first=True)
            for n in range(4):
                for h in range(2):
                    if (n, h) == (0, 1):
                        act.wait_ge(roped, PAIRS + KT)
                    step(n, n % 2, h, first=(n == 0 and h == 0), second=(n in (1, 2)))
            with by_two(act, 4, UNITS - 2) as n:
                for par in range(2):
                    for h in range(2):
                        step(n + par, par, h)
            for n in (UNITS - 2, UNITS - 1):
                for h in range(2):
                    step(n, n % 2, h, last=(n == UNITS - 1))
            move_lo(2 * UNITS - 2)
            pt_high(2 * UNITS - 1)
            gate(UNITS - 1, 1, first=False)
            move_lo(2 * UNITS - 1)

            with act.Fori(0, KT) as f:
                act.wait_ge(conv_gated, f + 1)
                copy(c_hi[:, bass.ds(f, 1), :].rearrange("p a s -> p (a s)"), work_c[:], c_hi_ready)
            act.wait_ge(tile_done, T_CO)
            act.wait_ge(attn_stored, 2 * UNITS)
            for n in range(KT):
                copy(blocks(h_hi[:, n, :]), feature_tile(n), h_hi_ready)
            with act.Fori(0, KT) as n:
                act.wait_ge(branches_added, n + 1)
                copy(c_hi[:, bass.ds(n, 1), :].rearrange("p a s -> p (a s)"), work_c[:], c_hi_ready)
            for n in range(KT):
                act.wait_ge(psum_read, T_WO + n + 1)
                nc.scalar.activation(h_hi[:, n, :], residual(n), ACT.Copy, scale=gain[:, KT + n:KT + n + 1]
                                     ).then_inc(h_hi_ready, 1)
                if n:
                    act.wait_ge(square_added, KT + n)
                nc.scalar.activation(work_c[:], residual(n), ACT.Square).then_inc(square_ready, 1)
            rms(2)
            f_base = 0
            for c, width in enumerate(CHUNKS):
                with act.Fori(0, width) as f:
                    act.wait_ge(psum_read, f * 2 + (T_UP[c] + 1))
                    nc.scalar.activation(work_b[:, 0:S], work_a[:], ACT.Tanh, scale=0.5).then_inc(silu_tanh, 1)
                    act.wait_ge(ffn_act, f + (f_base + 1))
                    copy(c_hi[:, bass.ds(f, 1), :].rearrange("p a s -> p (a s)"), work_c[:], c_hi_ready)
                f_base += width

            def final_rms(p):
                a, b = PIECES[p]
                act.wait_ge(mean_done, 3 + p)
                nc.scalar.activation(rstd[:, a:b], scores_ps[:, a:b], ACT.Sqrt, bias=eps[:]
                                     ).then_inc(rms_ready, 1)

            i = 0
            for p, (a, b) in enumerate(PIECES):
                for n in range(KT):
                    act.wait_ge(psum_read, T_DOWN[-1] + i + 1)
                    if i >= 2:
                        act.wait_ge(square_added, 2 * KT + i - 1)
                    nc.scalar.activation(final_square(i, b - a), residual(n)[:, a:b], ACT.Square
                                         ).then_inc(square_ready, 1)
                    act.wait_ge(square_ready, 2 * KT + i + 1)
                    nc.scalar.activation(residual(n)[:, a:b], residual(n)[:, a:b], ACT.Copy,
                                         scale=gain[:, 2 * KT + n:2 * KT + n + 1]).then_inc(y_scaled, 1)
                    if p > 0 and n == 2:
                        final_rms(p - 1)
                    i += 1
                act.wait_ge(square_added, 2 * KT + i)
                copy(ssq_hi[:, a:b], rstd_sq[:, a:b], ssq_split)
            final_rms(LAST_PIECE)

        @block.vector
        def _(dve):
            V = nc.vector

            def leave_psum(out, in1, t_plus_1, slot, ps=None):
                dve.wait_ge(tile_done, t_plus_1)
                V.tensor_tensor(out, (ps or slot_ps[slot])[:], in1, ALU.mult).then_inc(psum_read, 1)

            def lo_half(out, whole, hi, done):
                return V.tensor_tensor(out, whole, hi.bitcast(F32), ALU.subtract).then_inc(done, 1)

            def add_square(k, n, src):
                dve.wait_ge(square_ready, n * KT + k + 1)
                if k == 0:
                    V.tensor_copy(rstd_sq[:], src).then_inc(square_added, 1)
                else:
                    dve.wait_ge(square_added, n * KT + k)
                    V.tensor_tensor(rstd_sq[:], rstd_sq[:], src, ALU.add).then_inc(square_added, 1)

            def norm(n):
                if n > 1:
                    dve.wait_ge(ssq_split, 2 * n - 1)
                    lo_half(ssq_lo[:], rstd_sq[:], ssq_hi[:], ssq_split)
                dve.wait_ge(rms_ready, n)
                V.reciprocal(rstd[:], rstd[:]).then_inc(rstd_ready, 1)
                dve.wait_ge(rstd_ready, n)

            dve.wait_ge(setup_done, 5)
            dve.wait_ge(table_loaded, 1)
            dve.wait_ge(gains_loaded, 16)
            for k in range(KT):
                dve.wait_ge(x_loaded[x_load_of(k)], 16)
                dve.wait_ge(h_hi_ready, k + 1)
                V.scalar_tensor_tensor(h_lo[:, k, :], residual(k), gain[:, k:k + 1],
                                       h_hi[:, k, :].bitcast(F32), ALU.mult, ALU.subtract
                                       ).then_inc(h_lo_ready, 1)
            for k in range(KT):
                add_square(k, 0, square_buf[k % 2][:, 0:S])
            dve.wait_ge(square_added, KT)
            dve.wait_ge(ssq_split, 1)
            lo_half(ssq_lo[:], rstd_sq[:], ssq_hi[:], ssq_split)
            dve.wait_ge(consts_loaded, 16 * N_CONSTS)
            V.tensor_copy(take_cur[:].rearrange("p (t k) -> p t k", t=GROUP),
                          prob[:, 0, :].unsqueeze(1).to_broadcast([P, GROUP, P])).then_inc(mask_ready, 1)
            V.tensor_copy(prev_bias[:], bias_table[:, 0:1]).then_inc(bias_set, 1)
            norm(1)
            for i in range(PAIRS):
                leave_psum(v_feature[i][:], rstd[:], T_V + i + 1, i % 2)
            V.tensor_tensor(rstd_sq[:], rstd[:], rstd[:], ALU.mult).then_inc(rstd_sq_ready, 1)

            swap = [i ^ (ROT // 2) if i < ROT else i for i in range(32)]

            def rope(i, t_plus_1, slot, dst, first=False, ps=None):
                leave_psum(work_a[:], rstd[:], t_plus_1, slot, ps)
                if not first:
                    dve.wait_ge(roped, i)
                dve.wait_ge(psum_read, t_plus_1)
                V.stream_shuffle(work_b[:, 0:S], work_a[:], swap).then_inc(swapped, 1)
                V.tensor_tensor(work_c[:], work_a[:], rope_cos[:], ALU.mult).then_inc(cos_part, 1)
                dve.wait_ge(swapped, i + 1)
                V.tensor_tensor(work_b[:, 0:S], work_b[:, 0:S], rope_sin[:], ALU.mult).then_inc(sin_part, 1)
                dve.wait_ge(cos_part, i + 1)
                dve.wait_ge(sin_part, i + 1)
                c, b = work_c[:], work_b[:, 0:S]
                if len(dst.shape) == 3:
                    c, b = blocks(c), blocks(b)
                V.tensor_tensor(dst, c, b, ALU.add).then_inc(roped, 1)

            for i in range(PAIRS):
                rope(i, T_K + i + 1, i % 2, keys[:, P + i * S:P + (i + 1) * S], first=(i == 0),
                     ps=spare_ps if i == 0 else None)

            for i in range(KT):
                rope(PAIRS + i, T_Q + i + 1, i % 2, feature_tile(i))

            dve.wait_ge(mask_ready, 1)

            def begin_softmax(u):
                dve.wait_ge(prev_copied, u + 1)
                V.tensor_scalar(prev_bias[:], bias_table[:, bass.ds(u + 1, 1)], 1.0, None, ALU.mult
                                ).then_inc(bias_set, 1)
                by_head = scores_ps[:].rearrange("p (t w k) -> p t w k", t=GROUP, w=2)
                V.copy_predicated(scores[:], take_cur[:].rearrange("p (t k) -> p t k", t=GROUP),
                                  by_head[:, :, 1, :]).then_inc(scores_merged, 1)
                dve.wait_ge(scores_merged, u + 1)
                V.tensor_reduce(row_max[:], scores[:], AX.X, ALU.max).then_inc(max_ready, 1)
                dve.wait_ge(max_ready, u + 1)
                V.scalar_tensor_tensor(top[:], row_max[:], SCALE, sink[:, bass.ds(u * GROUP, GROUP)],
                                       ALU.mult, ALU.max).then_inc(top_ready, 1)
                dve.wait_ge(top_ready, u + 1)
                V.tensor_scalar(neg_max[:], top[:], -1.0, None, ALU.mult).then_inc(shift_ready, 1)
                V.tensor_tensor(sink_arg[:], sink[:, bass.ds(u * GROUP, GROUP)], top[:], ALU.subtract
                                ).then_inc(sink_arg_ready, 1)

            def end_softmax(u):
                dve.wait_ge(exp_done, u * (GROUP + 1) + (GROUP + 1))
                V.tensor_tensor(denom[:], exp_sum[:], sink_exp[:], ALU.add).then_inc(denom_ready, 1)
                dve.wait_ge(denom_ready, u + 1)
                V.reciprocal(inv_denom[:], denom[:]).then_inc(inv_ready, 1)
                dve.wait_ge(inv_ready, u + 1)
                V.tensor_tensor(prob[:], prob[:], inv_denom[:].unsqueeze(2).to_broadcast([P, GROUP, P]),
                                ALU.mult).then_inc(probs_ready, 1)

            def mask_probs(u, first=False):
                dve.wait_ge(probs_turned, u + 1)
                if not first:
                    dve.wait_ge(pt_lo_ready, u * 2)
                by_head = turn_ps.rearrange("p (t q) -> p t q", t=GROUP)
                V.tensor_tensor(pt_cur[:], by_head, keep_cur[:].unsqueeze(1).to_broadcast([P, GROUP, P]),
                                ALU.mult).then_inc(pt_masked, 1)
                dve.wait_ge(pt_masked, u * 2 + 1)
                V.tensor_tensor(pt_prev[:], by_head, pt_cur[:], ALU.subtract).then_inc(pt_masked, 1)

            def pt_low(u):
                for i, pt in enumerate((pt_cur, pt_prev)):
                    dve.wait_ge(pt_hi_ready, u * 2 + (i + 1))
                    lo_half(pt_lo[i][:], pt[:].rearrange("p t q -> p (t q)"), pt_hi[i][:], pt_lo_ready)

            def store_attention(n, h, u):
                rows = slice(h * HEAD, (h + 1) * HEAD)
                dve.wait_ge(pv_done, u + 1)
                dve.wait_ge(lo_moved, u + 1)
                V.tensor_tensor(m[rows, bass.ds(n * (GROUP * P), GROUP * P)], attn_ps[0:HEAD, :],
                                of_lo[0:HEAD, :], ALU.add).then_inc(attn_stored, 1)

            def gate(n, par, first=False):
                if not first:
                    dve.wait_ge(gate_tanh, n)
                leave_psum(work_a[:], rstd[:], n + (T_GATE + 1), par)

            def step(n, par, h, first=0, last=False):
                u = n * 2 + h
                begin_softmax(u)
                if first != 1:
                    mask_probs(u - 1, first=(first == 2))
                if not first:
                    store_attention(n - 1, h, u - 2)
                end_softmax(u)
                if first != 1:
                    pt_low(u - 1)
                if h == 0 and first != 1:
                    gate(n - 1, 1 - par, first=(isinstance(n, int) and n == 1))

            for h in range(2):
                step(0, 0, h, first=h + 1)
            for h in range(2):
                step(1, 1, h)
            with by_two(dve, 2, UNITS - 2) as n:
                for par in range(2):
                    for h in range(2):
                        step(n + par, par, h)
            for n in (UNITS - 2, UNITS - 1):
                for h in range(2):
                    step(n, n % 2, h, last=(n == UNITS - 1))
            last = 2 * UNITS - 1
            mask_probs(last)
            store_attention(UNITS - 1, 0, last - 1)
            pt_low(last)
            gate(UNITS - 1, 1)
            store_attention(UNITS - 1, 1, last)

            padded = work_b
            dve.wait_ge(gate_tanh, UNITS)
            dve.wait_ge(gate_stored[0], 16 * KT)
            dve.wait_ge(gate_stored[1], 16 * KT)
            V.memset(padded[:, 0:2], 0.0).then_inc(setup_done, 1)

            def conv(f, slot):
                t = f * 3 + T_CONV

                leave_psum(work_a[:], rstd_sq[:], t + 1, slot)
                dve.wait_ge(psum_read, t + 1)
                leave_psum(padded[:, 2:S + 2], work_a[:], t + 2, 1 - slot)
                dve.wait_ge(psum_read, t + 2)
                tap = lambda j: taps[:, bass.ds(f * 3 + j, 1)]
                V.tensor_scalar(work_c[:], padded[:, 2:S + 2], tap(2), None, ALU.mult).then_inc(conv_tap, 1)
                for j in (1, 0):
                    dve.wait_ge(conv_tap, f * 3 + (2 - j))
                    V.scalar_tensor_tensor(work_c[:], padded[:, j:S + j], tap(j), work_c[:],
                                           ALU.mult, ALU.add).then_inc(conv_tap, 1)
                leave_psum(work_a[:], rstd[:], t + 3, slot)
                dve.wait_ge(psum_read, t + 3)
                dve.wait_ge(conv_tap, f * 3 + 3)
                V.tensor_tensor(work_c[:], work_c[:], work_a[:], ALU.mult).then_inc(conv_gated, 1)
                dve.wait_ge(c_hi_ready, f + 1)
                lo_half(c_lo[:, bass.ds(f, 1), :].rearrange("p a s -> p (a s)"), work_c[:],
                        c_hi[:, bass.ds(f, 1), :].rearrange("p a s -> p (a s)"), c_lo_ready)
                dve.wait_ge(c_lo_ready, f + 1)

            dve.wait_ge(setup_done, 6)
            with by_two(dve, 0, KT) as f:
                conv(f, 0)
                conv(f + 1, 1)

            for n in range(KT):
                dve.wait_ge(h_hi_ready, KT + n + 1)
                lo_half(blocks(h_lo[:, n, :]), feature_tile(n), blocks(h_hi[:, n, :]), h_lo_ready)
            for n in range(KT):
                dve.wait_ge(gate_loaded[n % 2], 16 * (n // 2 + 1))
                dve.wait_ge(tile_done, T_CO + n + 1)
                dve.wait_ge(h_lo_ready, 2 * KT)
                V.scalar_tensor_tensor(feature_tile(n), blocks(reload_buf[n % 2][:, 0:S]), 1.0,
                                       blocks(slot_ps[n % 2][:]), ALU.add, ALU.mult).then_inc(psum_read, 1)
            for n in range(KT):
                g = KT + n
                dve.wait_ge(gate_loaded[g % 2], 16 * (g // 2 + 1))
                dve.wait_ge(tile_done, T_AO + n + 1)
                dve.wait_ge(c_lo_ready, KT + n)
                V.scalar_tensor_tensor(work_c[:], reload_buf[g % 2][:, 0:S], 1.0, slot_ps[n % 2][:],
                                       ALU.add, ALU.mult).then_inc(psum_read, 1)
                dve.wait_ge(psum_read, T_AO + n + 1)
                V.tensor_tensor(blocks(work_c[:]), blocks(work_c[:]), feature_tile(n), ALU.add
                                ).then_inc(branches_added, 1)
                dve.wait_ge(c_hi_ready, KT + n + 1)
                lo_half(c_lo[:, n, :], work_c[:], c_hi[:, n, :], c_lo_ready)
            for n in range(KT):
                dve.wait_ge(x_reloaded[n % 2], 16 * (n // 2 + 1))
                dve.wait_ge(tile_done, T_WO + n + 1)
                dve.wait_ge(branches_added, KT)
                V.scalar_tensor_tensor(residual(n), slot_ps[n % 2][:], 0.5, reload_buf[n % 2][:, 0:S],
                                       ALU.mult, ALU.add).then_inc(psum_read, 1)
                dve.wait_ge(h_hi_ready, 2 * KT + n + 1)
                dve.wait_ge(psum_read, T_WO + n + 1)
                V.scalar_tensor_tensor(h_lo[:, n, :], residual(n), gain[:, KT + n:KT + n + 1],
                                       h_hi[:, n, :].bitcast(F32), ALU.mult, ALU.subtract
                                       ).then_inc(h_lo_ready, 1)
                add_square(n, 1, work_c[:])
            dve.wait_ge(square_added, 2 * KT)
            norm(2)

            f_base = 0
            for c, width in enumerate(CHUNKS):
                with dve.Fori(0, width) as f:
                    t = f * 2 + T_UP[c]
                    leave_psum(work_a[:], rstd[:], t + 1, 0)
                    dve.wait_ge(psum_read, t + 1)
                    dve.wait_ge(silu_tanh, f + (f_base + 1))
                    V.scalar_tensor_tensor(work_c[:], work_b[:, 0:S], 1.0, work_a[:], ALU.add, ALU.mult
                                           ).then_inc(silu_gate, 1)
                    dve.wait_ge(silu_gate, f + (f_base + 1))
                    leave_psum(work_a[:], rstd[:], t + 2, 1)
                    dve.wait_ge(psum_read, t + 2)
                    V.tensor_tensor(work_c[:], work_c[:], work_a[:], ALU.mult).then_inc(ffn_act, 1)
                    dve.wait_ge(ffn_act, f + (f_base + 1))
                    dve.wait_ge(c_hi_ready, f + (2 * KT + f_base + 1))
                    lo_half(c_lo[:, bass.ds(f, 1), :].rearrange("p a s -> p (a s)"), work_c[:],
                            c_hi[:, bass.ds(f, 1), :].rearrange("p a s -> p (a s)"), c_lo_ready)
                    dve.wait_ge(c_lo_ready, f + (2 * KT + f_base + 1))
                f_base += width
                final = c == len(CHUNKS) - 1
                if not final:
                    with by_two(dve, 0, KT) as n:
                        for j in range(2):
                            dve.wait_ge(tile_done, n + (T_DOWN[c] + j + 1))
                            acc = m[:, bass.ds(n * S + j * S, S)]
                            V.scalar_tensor_tensor(acc, slot_ps[j][:], 0.5, acc, ALU.mult, ALU.add
                                                   ).then_inc(psum_read, 1)

            def final_rstd(p, a):
                dve.wait_ge(rms_ready, 3 + p)
                V.reciprocal(rstd[:, a:a + RECIP], rstd[:, a:a + RECIP]).then_inc(rstd_ready, 1)

            i = 0
            for p, (a, b) in enumerate(PIECES):
                for n in range(KT):
                    dve.wait_ge(tile_done, T_DOWN[-1] + i + 1)
                    V.scalar_tensor_tensor(residual(n)[:, a:b], slot_ps[i % 2][:, a:b], 0.5,
                                           residual(n)[:, a:b], ALU.mult, ALU.add).then_inc(psum_read, 1)
                    dve.wait_ge(square_ready, 2 * KT + i + 1)
                    if n == 0:
                        V.tensor_copy(rstd_sq[:, a:b], final_square(i, b - a)).then_inc(square_added, 1)
                    else:
                        dve.wait_ge(square_added, 2 * KT + i)
                        V.tensor_tensor(rstd_sq[:, a:b], rstd_sq[:, a:b], final_square(i, b - a), ALU.add
                                        ).then_inc(square_added, 1)
                    if p > 0:
                        first, end = PIECES[p - 1]
                        if 3 <= n < 3 + (end - first) // RECIP:
                            final_rstd(p - 1, first + (n - 3) * RECIP)
                    i += 1
                dve.wait_ge(ssq_split, 5 + 2 * p)
                lo_half(ssq_lo[:, a:b], rstd_sq[:, a:b], ssq_hi[:, a:b], ssq_split)
            a, b = PIECES[-1]
            for first in range(a, b, RECIP):
                final_rstd(LAST_PIECE, first)
            dve.wait_ge(rstd_ready, rstd_count(LAST_PIECE))
            for n in range(KT - POOL_OUT):
                dve.wait_ge(y_scaled, LAST_PIECE * KT + n + 1)
                y = residual(n)[:, a:b]
                V.tensor_tensor(y, y, rstd[:, a:b], ALU.mult).then_inc(out_dve, 1)


def shape_constants():
    f32 = np.float32
    j = np.arange(P)
    keep_cur = (j[:, None] <= j[None, :]).astype(f32)
    take_cur = (j[None, :] <= j[:, None]).astype(f32)
    bias_table = np.zeros((P, 2 * UNITS + 1), f32)
    bias_table[:, 0:-1:2 * NB] = bias_table[:, 1:-1:2 * NB] = NEG
    inv_freq = f32(500000.0) ** (-np.arange(0, ROT, 2, dtype=f32) / f32(ROT))
    angle = np.arange(S, dtype=f32)[None, :] * inv_freq[:, None].astype(f32)
    cos, sin = np.cos(angle).astype(f32), np.sin(angle).astype(f32)
    rope_cos, rope_sin = np.ones((P, S), f32), np.zeros((P, S), f32)
    for h in range(P // HEAD):
        a, half = h * HEAD, ROT // 2
        rope_cos[a:a + half] = rope_cos[a + half:a + ROT] = cos
        rope_sin[a:a + half], rope_sin[a + half:a + ROT] = -sin, sin
    return {"ident": np.eye(P, dtype=f32), "keep_cur": keep_cur, "take_cur": take_cur, "bias_table": bias_table, "rope_cos": rope_cos, "rope_sin": rope_sin}


def pack_weights(w_in, w_conv_out, w_attn_out, w_o, w_gate_up, w_down):
    def cols(w, first, n):
        v = w[:, first:first + n * P].reshape(-1, P, n, P)
        return v.transpose(2, 1, 0, 3)

    bounds = np.cumsum([0, D, D, D, D, N_KV * HEAD, N_KV * HEAD, D, D])
    cb, cc, cx, q, k, v, gate_c, gate_a = bounds[:-1]
    head_order = np.array([2 * GROUP * p + GROUP * e + t for p in range(PAIRS) for t in range(GROUP)
                           for e in range(2)])
    features = (head_order[:, None] * HEAD + np.arange(HEAD)[None, :]).ravel()
    conv = np.stack([cols(w_in, c, KT) for c in (cc, cx, cb)], 1).reshape(3 * KT, P, KT, P)
    parts = [cols(w_in, v, PAIRS), cols(w_in, k, PAIRS), cols(w_in[:, q:q + D][:, features], 0, KT),
             cols(w_in, gate_c, KT), cols(w_in, gate_a, KT), conv,
             cols(w_conv_out, 0, KT), cols(w_attn_out[features], 0, KT), cols(w_o, 0, KT)]
    f0 = 0
    for width in CHUNKS:
        gu = np.stack([cols(w_gate_up, f0 * P, width), cols(w_gate_up, D_FF + f0 * P, width)], 1)
        parts.append(gu.reshape(2 * width, P, KT, P))
        down = np.zeros((KT, P, KT, P), w_down.dtype)
        down[:, :, :width] = cols(w_down[f0 * P:(f0 + width) * P], 0, KT)
        parts.append(down)
        f0 += width
    return np.ascontiguousarray(np.concatenate(parts, 0).reshape(TILES, P, KT * P))


def kernel(x, g_mix, w_in, conv_w, attn_sinks, w_conv_out, w_attn_out, w_o, g_ffn, w_gate_up,
           w_down, g_final):
    import concourse.bacc as bacc
    from concourse.bass_utils import run_bass_kernel_spmd

    arr = np.asarray
    by_tile = lambda v: arr(v).reshape(-1, KT, P).transpose(2, 0, 1)
    s = arr(attn_sinks)[0].reshape(PAIRS, 1, 2, GROUP)
    s = np.broadcast_to(s, (PAIRS, NB, 2, GROUP)).reshape(1, -1)
    arrays = {
        "x_t": np.ascontiguousarray(arr(x)[0].T).reshape(KT, P, S),
        "w_stream": pack_weights(*(arr(w)[0] for w in (w_in, w_conv_out, w_attn_out, w_o, w_gate_up, w_down))),
        "gains": np.ascontiguousarray(np.concatenate(
            [by_tile(arr(g_mix)[0]), by_tile(arr(g_ffn)[0]), by_tile(arr(g_final))], 1).reshape(P, 3 * KT)),
        "conv_w": np.ascontiguousarray(by_tile(arr(conv_w)[0]).transpose(0, 2, 1).reshape(P, 3 * KT)),
        "sinks": np.ascontiguousarray(np.broadcast_to(s, (P, s.shape[1]))),
    }
    consts = shape_constants()
    nc = bacc.Bacc("TRN2", target_bir_lowering=False, num_devices=1)

    def dram(name, a):
        return nc.dram_tensor(name, a.shape, mybir.dt.from_np(a.dtype), kind="ExternalInput").ap()

    aps = {name: dram(name, a) for name, a in arrays.items()}
    const_aps = {name: dram("const_" + name, a) for name, a in consts.items()}
    out_t = nc.dram_tensor("out_t", (KT, P, S), F32, kind="ExternalOutput").ap()
    scratch = nc.dram_tensor("gate_scratch", (2 * KT, P, S), F32, kind="Internal").ap()
    block_kernel(nc, *(aps[n] for n in ("x_t", "w_stream", "gains", "conv_w", "sinks")), out_t,
                 const_aps, scratch)
    arrays.update({"const_" + name: a for name, a in consts.items()})
    r = run_bass_kernel_spmd(nc, [arrays], core_ids=[0])
    got = r.results[0]["out_t"]
    return np.ascontiguousarray(got.reshape(D, S).T).reshape(1, S, D)
```

```python
from contextlib import ExitStack, contextmanager

import numpy as np

import concourse.bass as bass
from concourse import mybir

F32 = mybir.dt.float32
F32R = mybir.dt.float32r
U8 = mybir.dt.uint8
ALU = mybir.AluOpType
ACT = mybir.ActivationFunctionType
AX = mybir.AxisListType

P = 128
D = 1024
S = 1024
KT = D // P
HALF = 512
HEAD = 64
N_HEADS = 16
N_KV = 4
GROUP = N_HEADS // N_KV
PAIRS = N_KV // 2
NB = S // P
UNITS = PAIRS * NB
D_FF = ((8 * D // 3 + 255) // 256) * 256
FT = D_FF // P
CHUNKS = (8, 8, 6)
ROT = HEAD // 4
SCALE = float(HEAD) ** -0.5
EPS = 1e-5
NEG = -1e30

T_V = 0
T_K = T_V + PAIRS
T_Q = T_K + PAIRS
T_GATE = T_Q + KT
T_CONV = T_GATE + 2 * KT
T_CO = T_CONV + 3 * KT
T_AO = T_CO + KT
T_WO = T_AO + KT
T_UP = []
T_DOWN = []
_t = T_WO + KT
for _f in CHUNKS:
    T_UP.append(_t)
    T_DOWN.append(_t + 2 * _f)
    _t += 2 * _f + KT
TILES = _t
assert sum(CHUNKS) == FT and TILES % 2 == 0


PIECES = ((0, 512), (512, 768), (768, 1024))
RECIP = 256

X_LOADS = ((0, 1), (1, 2), (2, 3), (3, 4), (4, 6), (6, 8))


def x_load_of(k):
    return next(i for i, (a, b) in enumerate(X_LOADS) if a <= k < b)


@contextmanager
def by_two(engine, first, last):
    with engine.Fori(0, (last - first) // 2) as i:
        yield i * 2 + first


def block_kernel(nc, x_t, w_stream, gains, conv_w, sinks, out_t, consts, gate_scratch):
    with ExitStack() as ctx:
        def sb(name, shape, dt=F32):
            return ctx.enter_context(nc.sbuf_tensor(name, shape, dt))

        def sem(name):
            return ctx.enter_context(nc.semaphore(name))

        def psum(name, shape):
            return ctx.enter_context(nc.psum_tensor(name, shape, F32))

        w_raw = [sb(f"w_raw{i}", [P, KT * P]) for i in range(2)]
        w_hi = [sb(f"w_hi{i}", [P, KT * P], F32R) for i in range(2)]
        w_lo = [sb(f"w_lo{i}", [P, KT * P], F32R) for i in range(2)]
        h_at = nc.sbuf_base
        h_hi = sb("h_hi", [P, KT, S], F32R)
        h_lo = sb("h_lo", [P, KT, S], F32R)
        m = sb("m", [P, KT * S])
        rstd = sb("rstd", [P, S])
        rstd_sq = sb("rstd_sq", [P, S])
        work_a = sb("work_a", [P, S])
        work_b_at = nc.sbuf_base
        work_b = sb("work_b", [P, S + 8])
        work_c_at = nc.sbuf_base
        work_c = sb("work_c", [P, S])
        ident = sb("ident", [P, P])
        mean_w = sb("mean_w", [P, P], F32R)
        keep_cur = sb("keep_cur", [P, P])
        take_cur = sb("take_cur", [P, GROUP * P], U8)
        bias_table = sb("bias_table", [P, 2 * UNITS + 1])
        prev_bias = sb("prev_bias", [P, 1])
        zero = sb("zero", [P, 1])
        gain = sb("gain", [P, 3 * KT])
        taps = sb("taps", [P, 3 * KT])
        sink = sb("sink", [P, 2 * UNITS * GROUP])
        eps = sb("eps", [P, 1])
        row_max = sb("row_max", [P, GROUP])
        top = sb("top", [P, GROUP])
        neg_max = sb("neg_max", [P, GROUP])
        sink_arg = sb("sink_arg", [P, GROUP])
        sink_exp = sb("sink_exp", [P, GROUP])
        exp_sum = sb("exp_sum", [P, GROUP])
        denom = sb("denom", [P, GROUP])
        inv_denom = sb("inv_denom", [P, GROUP])

        with ExitStack() as attention_only:
            def asb(name, shape, dt=F32):
                return attention_only.enter_context(nc.sbuf_tensor(name, shape, dt))

            rope_cos = asb("rope_cos", [P, S])
            rope_sin_at = nc.sbuf_base
            rope_sin = asb("rope_sin", [P, S])
            keys = asb("keys", [P, (UNITS + 1) * P])
            values = asb("values", [P, (UNITS + 1) * P])
            with ExitStack() as before_attention:
                v_feature = [before_attention.enter_context(nc.sbuf_tensor(f"v_feature{i}", [P, S], F32))
                             for i in range(PAIRS)]
            q_hi = asb("q_hi", [P, GROUP * P], F32R)
            q_lo = [asb(f"q_lo{i}", [P, GROUP * P], F32R) for i in range(2)]
            k_hi = asb("k_hi", [P, 2 * P], F32R)
            k_lo = asb("k_lo", [P, 2 * P], F32R)
            q_twice = [asb(f"q_twice{i}", [P, 2, GROUP * P], F32R) for i in range(2)]
            k_both = [asb(f"k_both{i}", [P, 2, 2 * P], F32R) for i in range(2)]
            v_both = [asb(f"v_both{i}", [P, 2, 2, 2, HEAD], F32R) for i in range(2)]
            scores = asb("scores", [P, GROUP, P])
            of_lo = asb("of_lo", [P, GROUP * P])
            prob = asb("prob", [P, GROUP, P])
            pt_cur = nc.alloc_sbuf_tensor_at("pt_cur", [P, GROUP, P], F32, offset=rope_sin_at)
            pt_prev = nc.alloc_sbuf_tensor_at("pt_prev", [P, GROUP, P], F32, offset=rope_sin_at + GROUP * P * 4)
            pt_hi = [asb(f"pt_hi{i}", [P, GROUP * P], F32R) for i in range(2)]
            pt_lo = [asb(f"pt_lo{i}", [P, GROUP * P], F32R) for i in range(2)]
        c_hi = sb("c_hi", [P, KT, S], F32R)
        c_lo = sb("c_lo", [P, KT, S], F32R)
        ssq_hi = nc.alloc_sbuf_tensor_at("ssq_hi", [P, S], F32R, offset=work_b_at)
        ssq_lo = nc.alloc_sbuf_tensor_at("ssq_lo", [P, S], F32R, offset=work_c_at)
        WD_COLS = CHUNKS[-1] * P
        wd_hi = nc.alloc_sbuf_tensor_at("wd_hi", [P, KT - 2, WD_COLS], F32R, offset=h_at)
        wd_lo = nc.alloc_sbuf_tensor_at("wd_lo", [P, KT - 2, WD_COLS], F32R, offset=h_at + KT * S * 4)

        slot_ps = [psum(f"slot_ps{i}", [P, S]) for i in range(2)]
        scores_ps = psum("scores_ps", [P, S])
        spare_ps = psum("spare_ps", [P, S])
        turn_ps = spare_ps[:, 0:GROUP * P]
        attn_ps = spare_ps[:, GROUP * P:2 * GROUP * P]

        def feature_tile(kt):
            pair, head = kt // GROUP, kt % GROUP
            v = m[:].rearrange("p (a b t q) -> p a b t q", a=PAIRS, b=NB, t=GROUP)
            return v[:, pair, :, head, :]

        def blocks(ap):
            return ap.rearrange("p (b q) -> p b q", b=NB)

        def residual(n):
            return m[:, n * S:(n + 1) * S]

        gains_loaded = sem("gains_loaded")
        consts_loaded = sem("consts_loaded")
        x_loaded = [sem(f"x_loaded{i}") for i in range(len(X_LOADS))]
        first_loaded = [sem(f"first_loaded{i}") for i in range(2)]
        raw_loaded = [sem(f"raw_loaded{i}") for i in range(2)]
        table_loaded = sem("table_loaded")
        first_hi = sem("first_hi")
        first_split = sem("first_split")
        raw_hi = sem("raw_hi")
        weights_split = sem("weights_split")
        setup_done = sem("setup_done")
        tile_done = sem("tile_done")
        psum_read = sem("psum_read")
        h_hi_ready = sem("h_hi_ready")
        h_lo_ready = sem("h_lo_ready")
        c_hi_ready = sem("c_hi_ready")
        c_lo_ready = sem("c_lo_ready")
        square_ready = sem("square_ready")
        square_added = sem("square_added")
        ssq_split = sem("ssq_split")
        mean_done = sem("mean_done")
        rms_ready = sem("rms_ready")
        rstd_ready = sem("rstd_ready")
        rstd_sq_ready = sem("rstd_sq_ready")
        swapped = sem("swapped")
        cos_part = sem("cos_part")
        sin_part = sem("sin_part")
        roped = sem("roped")
        v_turned = sem("v_turned")
        v_stored = sem("v_stored")
        unit_hi = sem("unit_hi")
        unit_lo = sem("unit_lo")
        unit_placed = sem("unit_placed")
        scores_done = sem("scores_done")
        mask_ready = sem("mask_ready")
        bias_set = sem("bias_set")
        prev_copied = sem("prev_copied")
        scores_merged = sem("scores_merged")
        max_ready = sem("max_ready")
        top_ready = sem("top_ready")
        shift_ready = sem("shift_ready")
        sink_arg_ready = sem("sink_arg_ready")
        exp_done = sem("exp_done")
        denom_ready = sem("denom_ready")
        inv_ready = sem("inv_ready")
        probs_ready = sem("probs_ready")
        probs_turned = sem("probs_turned")
        pt_masked = sem("pt_masked")
        pt_hi_ready = sem("pt_hi_ready")
        pt_lo_ready = sem("pt_lo_ready")
        pv_done = sem("pv_done")
        lo_moved = sem("lo_moved")
        attn_stored = sem("attn_stored")
        gate_tanh = sem("gate_tanh")
        gate_stored = [sem(f"gate_stored{i}") for i in range(2)]
        gate_loaded = [sem(f"gate_loaded{i}") for i in range(2)]
        conv_tap = sem("conv_tap")
        conv_gated = sem("conv_gated")
        branches_added = sem("branches_added")
        x_reloaded = [sem(f"x_reloaded{i}") for i in range(2)]
        silu_tanh = sem("silu_tanh")
        silu_gate = sem("silu_gate")
        ffn_act = sem("ffn_act")
        y_scaled = sem("y_scaled")
        out_dve = sem("out_dve")
        out_pool = sem("out_pool")
        out_stored = sem("out_stored")

        N_CONSTS = len(consts) + 2
        FIRST_PARTS = 4
        FIRST_COLS = KT * P // FIRST_PARTS
        WARM_UP = 12
        PLACE = 8 * 16
        own_rows = [slice(h * HEAD, (h + 1) * HEAD) for h in range(2)]
        other_rows = own_rows[::-1]
        POOL_OUT = 3
        LAST_PIECE = len(PIECES) - 1

        def scaled_by_pool(p, n):
            return p < LAST_PIECE or n >= KT - POOL_OUT

        def pool_scaled_before(p, n):
            return p * KT + (n if p < LAST_PIECE else n - (KT - POOL_OUT))

        def rstd_count(p):
            return 2 + PIECES[p][1] // RECIP

        gate_buf = [work_b, work_c]
        square_buf = [work_a, work_b]
        reload_buf = [work_a, work_b]

        final_ps = slot_ps + [spare_ps]

        def final_square(i, width):
            return work_a[:, i % 2 * HALF:i % 2 * HALF + width]

        block = ctx.enter_context(nc.Block())

        @block.sync
        def _(sp):
            def load_weights(t_expr, slot, count):
                if count is not None:
                    sp.wait_ge(weights_split, count - 2)
                sp.dma_start(w_raw[slot][:], w_stream[bass.ds(t_expr, 1), :, :].rearrange("a p n -> (a p) n")
                             ).then_inc(raw_loaded[slot], 16)

            def load_x(i):
                a, b = X_LOADS[i]
                sp.dma_start(m[:, a * S:b * S].rearrange("p (k s) -> p k s", s=S),
                             x_t[a:b].rearrange("k p s -> p k s")).then_inc(x_loaded[i], 16)

            def load_first_weights(t, cols, done):
                sp.dma_start(w_raw[t][:, cols], w_stream[t][:, cols]).then_inc(done[t], 16)

            sp.dma_start(gain[:], gains).then_inc(gains_loaded, 16)
            load_first_weights(0, slice(0, FIRST_COLS), first_loaded)
            load_x(0)
            load_first_weights(1, slice(0, FIRST_COLS), first_loaded)
            load_x(1)
            load_x(2)
            load_first_weights(0, slice(FIRST_COLS, KT * P), raw_loaded)
            load_first_weights(1, slice(FIRST_COLS, KT * P), raw_loaded)
            for i in range(3, len(X_LOADS)):
                load_x(i)
            for t in (2, 3):
                sp.wait_ge(first_split, 2 * (FIRST_PARTS - 1) + t - 1)
                load_weights(t, t % 2, None)
            for dst, src in ((taps, conv_w), (sink, sinks), (ident, consts["ident"]),
                             (keep_cur, consts["keep_cur"]),
                             (prob[:, 0, :], consts["take_cur"]), (bias_table, consts["bias_table"]),
                             (rope_cos, consts["rope_cos"]), (rope_sin, consts["rope_sin"])):
                sp.dma_start(dst[:], src).then_inc(consts_loaded, 16)

            def place(n, par, first=False):
                def move(to, what):
                    sp.dma_start(to.bitcast(F32), what.bitcast(F32)).then_inc(unit_placed, 16)

                sp.wait_ge(unit_hi, n * 3 + 2)
                if not first:
                    sp.wait_ge(scores_done, n * 2 + (-2))
                for h, rows in enumerate(own_rows):
                    for to_rows in own_rows:
                        move(q_twice[par][to_rows, h, :], q_hi[rows, :])
                    move(k_both[par][rows, h, :], k_hi[rows, :])
                sp.wait_ge(unit_lo, n * 3 + 2)
                for h, rows in enumerate(own_rows):
                    move(k_both[par][other_rows[h], h, :], k_lo[rows, :])

            def store_gate(n, par):
                sp.wait_ge(gate_tanh, n + 1)
                sp.dma_start(gate_scratch[bass.ds(n, 1), :, :].rearrange("a p n -> (a p) n"),
                             gate_buf[par][:, 0:S]).then_inc(gate_stored[par], 16)

            with by_two(sp, 4, T_GATE + 2) as t:
                for j in range(2):
                    load_weights(t + j, j, t + (j - 1))
            place(0, 0, first=True)
            for t in range(T_GATE + 2, T_GATE + 4):
                load_weights(t, t % 2, t - 1)
            place(1, 1, first=True)
            with by_two(sp, 1, UNITS - 1) as n:
                for j in range(2):
                    load_weights(n + (T_GATE + 3 + j), j, n + (T_GATE + 2 + j))
                    place(n + (j + 1), j)
                    store_gate(n + (j - 1), j)
            for n in range(UNITS - 1, UNITS + 1):
                load_weights(n + T_GATE + 3, (n - 1) % 2, n + T_GATE + 2)
                store_gate(n - 1, (n - 1) % 2)
            with by_two(sp, T_CONV + 4, T_CO + 2) as t:
                for j in range(2):
                    load_weights(t + j, j, t + (j - 1))
            for i in range(2):
                sp.wait_ge(gate_stored[i], 16 * KT)
            sp.wait_ge(conv_gated, KT)
            sp.wait_ge(conv_tap, 3 * KT)

            def reload(j, t, n, source, done):
                sp.wait_ge(psum_read, t - 1)
                sp.dma_start(reload_buf[j][:, 0:S], source[bass.ds(n, 1), :, :].rearrange("a p n -> (a p) n")
                             ).then_inc(done[j], 16)
                load_weights(t + 2, j, t + 1)

            with by_two(sp, 0, 2 * KT) as n:
                for j in range(2):
                    reload(j, n + (T_CO + j), n + j, gate_scratch, gate_loaded)
            with by_two(sp, 0, KT) as n:
                for j in range(2):
                    reload(j, n + (T_WO + j), n + j, x_t, x_reloaded)
            with by_two(sp, T_UP[0] + 2, TILES) as t:
                for j in range(2):
                    load_weights(t + j, j, t + (j - 1))
            for p, (a, b) in enumerate(PIECES):
                for n in range(KT):
                    if p == LAST_PIECE and scaled_by_pool(p, n):
                        continue
                    if scaled_by_pool(p, n):
                        sp.wait_ge(out_pool, pool_scaled_before(p, n) + 1)
                    else:
                        sp.wait_ge(out_dve, n + 1)
                    sp.dma_start(out_t[n][:, a:b], residual(n)[:, a:b]).then_inc(out_stored, 16)
            sp.wait_ge(out_stored, 16 * KT * len(PIECES))

        @block.gpsimd
        def _(pool):
            pool.memset(zero[:], 0.0).then_inc(setup_done, 1)
            pool.memset(mean_w[:].bitcast(F32), 1.0 / D).then_inc(setup_done, 1)
            pool.memset(eps[:], EPS).then_inc(setup_done, 1)
            pool.memset(keys[:, 0:P], 0.0).then_inc(setup_done, 1)
            pool.memset(values[:, 0:P], 0.0).then_inc(setup_done, 1)

            def split(slot, loads, t_plus_1, cols=KT * P):
                pool.wait_ge(raw_loaded[slot], loads)
                pool.wait_ge(tile_done, t_plus_1 - 2)
                hi, lo, raw = w_hi[slot][:, 0:cols], w_lo[slot][:, 0:cols], w_raw[slot][:, 0:cols]
                nc.gpsimd.tensor_tensor(hi, raw, zero[:].to_broadcast([P, cols]), ALU.add).then_inc(raw_hi, 1)
                pool.wait_ge(raw_hi, t_plus_1 - 2)
                nc.gpsimd.tensor_tensor(lo, raw, hi.bitcast(F32), ALU.subtract).then_inc(weights_split, 1)

            pool.wait_ge(setup_done, 1)
            for i in range(FIRST_PARTS):
                for t in range(2):
                    pool.wait_ge((first_loaded if i == 0 else raw_loaded)[t], 16)
                    part = slice(i * FIRST_COLS, (i + 1) * FIRST_COLS)
                    hi, lo, raw = w_hi[t][:, part], w_lo[t][:, part], w_raw[t][:, part]
                    nc.gpsimd.tensor_tensor(hi, raw, zero[:].to_broadcast([P, FIRST_COLS]),
                                            ALU.add).then_inc(first_hi, 1)
                    pool.wait_ge(first_hi, 2 * i + t + 1)
                    nc.gpsimd.tensor_tensor(lo, raw, hi.bitcast(F32), ALU.subtract).then_inc(first_split, 1)
            with pool.Fori(1, T_GATE // 2) as i:
                for j in range(2):
                    split(j, i * 16 + 16, i * 2 + (j + 1))

            def split_unit(n, par):
                v = values[:, bass.ds(n * P, 2 * P)].rearrange("p (x d) -> p x d", d=HEAD)
                v_by_head = [v_both[par][:, :, :, i, :].rearrange("p b h d -> p (b h) d") for i in range(2)]
                for i, (lo, whole, hi) in enumerate((
                        (q_lo[par][:], m[:, bass.ds(n * (GROUP * P), GROUP * P)], q_hi[:]),
                        (k_lo[:], keys[:, bass.ds(n * P, 2 * P)], k_hi[:]),
                        (v_by_head[1], v, v_by_head[0]))):
                    pool.wait_ge(unit_hi, n * 3 + (i + 1))
                    nc.gpsimd.tensor_tensor(lo, whole, hi.bitcast(F32), ALU.subtract).then_inc(unit_lo, 1)

            split_unit(0, 0)
            split(0, 8 * T_GATE + 16, T_GATE + 1)
            with by_two(pool, 0, UNITS - 2) as n:
                for j in range(2):
                    split(1 - j, n * 8 + (8 * T_GATE + 16 * (j + 1)), n + (T_GATE + j + 2))
                    split_unit(n + (j + 1), 1 - j)
            split(1, 8 * (T_CONV - 2) + 16, T_CONV)
            split_unit(UNITS - 1, 1)
            with pool.Fori(T_CONV // 2, T_DOWN[-1] // 2) as i:
                for j in range(2):
                    split(j, i * 16 + 16, i * 2 + (j + 1))
            for j in range(2):
                split(j, 8 * T_DOWN[-1] + 16, T_DOWN[-1] + j + 1, cols=WD_COLS)
            pool.wait_ge(tile_done, T_DOWN[-1])
            for n in range(2, KT):
                t = T_DOWN[-1] + n
                hi, lo, raw = wd_hi[:, n - 2, :], wd_lo[:, n - 2, :], w_raw[t % 2][:, 0:WD_COLS]
                pool.wait_ge(raw_loaded[t % 2], 16 * (t // 2 + 1))
                nc.gpsimd.tensor_tensor(hi, raw, zero[:].to_broadcast([P, WD_COLS]), ALU.add).then_inc(raw_hi, 1)
                pool.wait_ge(raw_hi, t - 1)
                nc.gpsimd.tensor_tensor(lo, raw, hi.bitcast(F32), ALU.subtract).then_inc(weights_split, 1)
            for p, (a, b) in enumerate(PIECES):
                pool.wait_ge(rstd_ready, rstd_count(p))
                for n in range(KT):
                    if scaled_by_pool(p, n):
                        pool.wait_ge(y_scaled, p * KT + n + 1)
                        y = residual(n)[:, a:b]
                        nc.gpsimd.tensor_tensor(y, y, rstd[:, a:b], ALU.mult).then_inc(out_pool, 1)

        @block.tensor
        def _(pe):
            def k_step(ps, slot, rhs, k, start, stop, halves=(0, 1), ready=None):
                for i, (w, r) in enumerate(((w_hi, rhs[0]), (w_lo, rhs[0]), (w_hi, rhs[1]))):
                    if ready is not None and i != 1:
                        pe.wait_ge(ready[i // 2], ready[2] + k + 1)
                    for s in halves:
                        cols = slice(s * HALF, (s + 1) * HALF)
                        last = nc.tensor.matmul(ps[:, cols], w[slot][:, k * P:(k + 1) * P],
                                                r[:, k, cols], start=(start and i == 0),
                                                stop=(stop and i == 2))
                return last

            def product(slot, rhs, k_tiles=KT, halves=(0, 1), ready=None, between=None, ps=None):
                ps = slot_ps[slot] if ps is None else ps
                for k in range(k_tiles):
                    last = k_step(ps, slot, rhs, k, k == 0, k == k_tiles - 1, halves, ready)
                    if between is not None and k in between:
                        between[k]()
                return last

            def slot_free(t_minus_1):
                pe.wait_ge(psum_read, t_minus_1)

            def tile(t, slot, rhs, **how):
                pe.wait_ge(weights_split, t + (-1))
                if "ps" not in how:
                    slot_free(t + (-1))
                product(slot, rhs, **how).then_inc(tile_done, 1)

            def tiles(first, last, rhs, k_tiles=KT, ready=None):
                with by_two(pe, first, last) as t:
                    tile(t, 0, rhs, k_tiles=k_tiles, ready=ready)
                    tile(t + 1, 1, rhs, k_tiles=k_tiles)

            def mean_square(n, pieces=((0, HALF), (HALF, S))):
                pe.wait_ge(ssq_split, 2 * n)
                for a, b in pieces:
                    cols = slice(a, b)
                    nc.tensor.matmul(scores_ps[:, cols], mean_w[:], ssq_hi[:, cols], start=True, stop=False)
                    last = nc.tensor.matmul(scores_ps[:, cols], mean_w[:], ssq_lo[:, cols],
                                            start=False, stop=True)
                last.then_inc(mean_done, 1)

            def turn_values(i):
                pe.wait_ge(psum_read, T_V + i + 1)
                if i:
                    pe.wait_ge(v_stored, i)
                else:
                    pe.wait_ge(psum_read, 4)
                for b in range(NB):
                    last = nc.tensor.transpose(scores_ps[:, b * P:(b + 1) * P],
                                               v_feature[i][:, b * P:(b + 1) * P], ident[:])
                last.then_inc(v_turned, 1)

            H = (h_hi, h_lo)
            C = (c_hi, c_lo)
            pe.wait_ge(setup_done, 2)
            for _ in range(WARM_UP):
                nc.tensor.matmul(spare_ps[:, 0:4 * P], mean_w[:],
                                 mean_w[:].unsqueeze(1).to_broadcast([P, 4, P]), start=True, stop=True)
            half = KT // 2
            for t, k in ([(t, k) for k in range(half) for t in range(2)]
                         + [(t, k) for t in range(2) for k in range(half, KT)]):
                if k % (KT // FIRST_PARTS) == 0:
                    pe.wait_ge(first_split, k // (KT // FIRST_PARTS) * 2 + t + 1)
                last = k_step(slot_ps[t], t, H, k, k == 0, k == KT - 1,
                              ready=(h_hi_ready, h_lo_ready, 0) if t == 0 else None)
                if k == KT - 1:
                    last.then_inc(tile_done, 1)
            tile(2, 0, H, ps=spare_ps, between={4: lambda: mean_square(1)})
            pe.wait_ge(rms_ready, 1)
            tile(3, 1, H, ps=scores_ps)
            tile(4, 0, H)
            pe.wait_ge(consts_loaded, 16 * N_CONSTS)
            tile(5, 1, H, between={0: lambda: turn_values(0), 4: lambda: turn_values(1)})
            tiles(6, T_GATE - 2, H)
            tile(T_GATE - 2, 0, H)

            def score(n, par, h):
                u = n * 2 + h
                if h == 0:
                    pe.wait_ge(unit_lo, n * 3 + 1)
                    pe.wait_ge(unit_placed, n * PLACE + PLACE)
                if not isinstance(u, int) or u > 0:
                    pe.wait_ge(scores_merged, u)
                rows = own_rows[h]
                for t in range(GROUP):
                    dst = scores_ps[:, t * 2 * P:(t + 1) * 2 * P]
                    q_cols = slice(t * P, (t + 1) * P)
                    nc.tensor.matmul(dst, q_twice[par][:, h, q_cols], k_both[par][:, h, :],
                                     start=True, stop=False)
                    last = nc.tensor.matmul(dst, q_lo[par][rows, q_cols], k_both[par][rows, h, :],
                                            start=False, stop=True)
                last.then_inc(scores_done, 1)

            def turn_probs(u):
                pe.wait_ge(probs_ready, u + 1)
                if not isinstance(u, int) or u > 0:
                    pe.wait_ge(pt_masked, u * 2)
                for t in range(GROUP):
                    last = nc.tensor.transpose(turn_ps[:, t * P:(t + 1) * P], prob[:, t, :], ident[:])
                last.then_inc(probs_turned, 1)

            def weigh_values(par, h, u):
                pe.wait_ge(pt_hi_ready, u * 2 + 2)
                pe.wait_ge(pt_lo_ready, u * 2 + 2)
                if not isinstance(u, int) or u > 0:
                    pe.wait_ge(attn_stored, u)
                n = 0
                for pt_of, v_block in ((0, 1), (1, 0)):
                    v = v_both[par][:, v_block, h].rearrange("p a d -> p (a d)")
                    for p in (pt_hi, pt_lo):
                        last = nc.tensor.matmul(attn_ps, v, p[pt_of][:], start=(n == 0), stop=(n == 3))
                        n += 1
                last.then_inc(pv_done, 1)

            def attention_step(n, par, h, first_unit=False):
                u = n * 2 + h
                if not (first_unit and h == 0):
                    score(n, par, h)
                if not first_unit:
                    if h == 0:
                        pe.wait_ge(unit_hi, n * 3)
                        pe.wait_ge(unit_lo, n * 3)
                    weigh_values(1 - par, h, u - 2)
                if not (first_unit and h == 0):
                    turn_probs(u - 1)
                if h == 0:
                    pe.wait_ge(weights_split, n + (T_GATE - 1))
                    slot_free(n + (T_GATE - 1))
                done = product(par, H, halves=(h,))
                if h == 1:
                    done.then_inc(tile_done, 1)

            tile(T_GATE - 1, 1, H, between={3: lambda: score(0, 0, 0)})
            for n in range(2):
                for h in range(2):
                    attention_step(n, n, h, first_unit=(n == 0))
            with by_two(pe, 2, UNITS) as n:
                for par in range(2):
                    for h in range(2):
                        attention_step(n + par, par, h)
            pe.wait_ge(unit_hi, 3 * UNITS)
            pe.wait_ge(unit_lo, 3 * UNITS)
            weigh_values(1, 0, 2 * UNITS - 2)
            turn_probs(2 * UNITS - 1)
            tile(T_CONV, 0, H)
            weigh_values(1, 1, 2 * UNITS - 1)
            tile(T_CONV + 1, 1, H)
            tiles(T_CONV + 2, T_CO, H)
            tiles(T_CO, T_AO, C, ready=(c_hi_ready, c_lo_ready, 0))
            tiles(T_AO, T_WO, H, ready=(h_hi_ready, h_lo_ready, KT))
            tiles(T_WO, T_UP[0], C, ready=(c_hi_ready, c_lo_ready, KT))
            c_base = 2 * KT
            for c, width in enumerate(CHUNKS):
                if c == 0:
                    tile(T_UP[0], 0, H, ready=(h_hi_ready, h_lo_ready, 2 * KT))
                    tile(T_UP[0] + 1, 1, H, between={3: lambda: mean_square(2)})
                    pe.wait_ge(attn_stored, 2 * UNITS)
                    tile(T_UP[0] + 2, 0, H, ps=spare_ps)
                    tile(T_UP[0] + 3, 1, H)
                    tiles(T_UP[0] + 4, T_DOWN[0], H)
                else:
                    tiles(T_UP[c], T_DOWN[c], H)
                if c < len(CHUNKS) - 1:
                    tiles(T_DOWN[c], T_DOWN[c] + KT, C, k_tiles=width, ready=(c_hi_ready, c_lo_ready, c_base))
                    c_base += width

            def down(i, k_tiles):
                (a, b), n = PIECES[i // KT], i % KT
                hi, lo = (w_hi[n], w_lo[n]) if n < 2 else (wd_hi[:, n - 2, :], wd_lo[:, n - 2, :])
                for k in k_tiles:
                    rows = slice(k * P, (k + 1) * P)
                    for j, (w, c) in enumerate(((hi, c_hi), (hi, c_lo), (lo, c_hi))):
                        last = nc.tensor.matmul(final_ps[i % 3][:, a:b], w[:, rows], c[:, k, a:b],
                                                start=(k == 0 and j == 0), stop=(k == width - 1 and j == 2))
                return last

            for i in range(2):
                pe.wait_ge(weights_split, T_DOWN[-1] + i - 1)
                slot_free(T_DOWN[-1] + i - 1)
                if i == 0:
                    pe.wait_ge(c_hi_ready, c_base + width - 1)
                    pe.wait_ge(c_lo_ready, c_base + width - 1)
                down(i, range(width - 1))
            pe.wait_ge(c_hi_ready, c_base + width)
            pe.wait_ge(c_lo_ready, c_base + width)
            for i in range(2):
                down(i, (width - 1,)).then_inc(tile_done, 1)
            for i in range(2, KT * len(PIECES)):
                if i < KT:
                    pe.wait_ge(weights_split, T_DOWN[-1] + i - 1)
                pe.wait_ge(psum_read, T_DOWN[-1] + i - 2)
                down(i, range(width)).then_inc(tile_done, 1)
                p, n = i // KT, i % KT
                if p > 0 and n == 1:
                    mean_square(2 + p, (PIECES[p - 1],))
            mean_square(3 + LAST_PIECE, (PIECES[-1],))

        @block.scalar
        def _(act):

            def copy(dst, src, done):
                return nc.scalar.activation(dst, src, ACT.Copy).then_inc(done, 1)

            act.wait_ge(setup_done, 5)
            copy(inv_denom[:, 0:1], zero[:], table_loaded)
            act.wait_ge(gains_loaded, 16)
            for k in range(KT):
                act.wait_ge(x_loaded[x_load_of(k)], 16)
                nc.scalar.activation(h_hi[:, k, :], residual(k), ACT.Copy, scale=gain[:, k:k + 1]
                                     ).then_inc(h_hi_ready, 1)

            def rms(n):
                act.wait_ge(square_added, n * KT)
                copy(ssq_hi[:], rstd_sq[:], ssq_split)
                act.wait_ge(mean_done, n)
                nc.scalar.activation(rstd[:], scores_ps[:], ACT.Sqrt, bias=eps[:]).then_inc(rms_ready, 1)

            for k in range(KT):
                if k >= 2:
                    act.wait_ge(square_added, k - 1)
                nc.scalar.activation(square_buf[k % 2][:, 0:S], residual(k), ACT.Square
                                     ).then_inc(square_ready, 1)
            rms(1)
            for i in range(PAIRS):
                act.wait_ge(v_turned, i + 1)
                copy(values[:, P + i * S:P + (i + 1) * S], scores_ps[:], v_stored)

            def split_qk(n, first=False):
                if not first:
                    act.wait_ge(unit_placed, n * PLACE)
                copy(q_hi[:], m[:, bass.ds(n * (GROUP * P), GROUP * P)], unit_hi)
                copy(k_hi[:], keys[:, bass.ds(n * P, 2 * P)], unit_hi)

            def split_v(n, par, first=False):
                if not first:
                    act.wait_ge(pv_done, n * 2 + (-2))
                copy(v_both[par][:, :, :, 0, :].rearrange("p b h d -> p (b h) d"),
                     values[:, bass.ds(n * P, 2 * P)].rearrange("p (x d) -> p x d", d=HEAD), unit_hi)

            act.wait_ge(mask_ready, 1)

            def softmax(u, before_exp=None):
                act.wait_ge(scores_done, u + 1)
                if not isinstance(u, int) or u > 0:
                    act.wait_ge(exp_done, u * (GROUP + 1))
                act.wait_ge(bias_set, u + 1)
                by_head = scores_ps[:].rearrange("p (t w k) -> p t w k", t=GROUP, w=2)
                nc.scalar.activation(scores[:], by_head[:, :, 0, :], ACT.Identity,
                                     bias=prev_bias[:]).then_inc(prev_copied, 1)
                if before_exp is not None:
                    before_exp()
                act.wait_ge(shift_ready, u + 1)
                if not isinstance(u, int) or u > 0:
                    act.wait_ge(probs_turned, u)
                    act.wait_ge(denom_ready, u)
                for t in range(GROUP):
                    nc.scalar.activation(prob[:, t, :], scores[:, t, :], ACT.Exp, bias=neg_max[:, t:t + 1],
                                         scale=SCALE, accum_out=exp_sum[:, t:t + 1]).then_inc(exp_done, 1)
                act.wait_ge(sink_arg_ready, u + 1)
                nc.scalar.activation(sink_exp[:], sink_arg[:], ACT.Exp).then_inc(exp_done, 1)

            def move_lo(u):
                act.wait_ge(pv_done, u + 1)
                if not isinstance(u, int) or u > 0:
                    act.wait_ge(attn_stored, u)
                copy(of_lo[0:HEAD, :], attn_ps[HEAD:2 * HEAD, :], lo_moved)

            def pt_high(u):
                if not isinstance(u, int) or u > 0:
                    act.wait_ge(pv_done, u)
                for i, pt in enumerate((pt_cur, pt_prev)):
                    act.wait_ge(pt_masked, u * 2 + (i + 1))
                    copy(pt_hi[i][:], pt[:].rearrange("p t q -> p (t q)"), pt_hi_ready)

            def gate(n, par, first):
                act.wait_ge(psum_read, n + (T_GATE + 1))
                if not first:
                    act.wait_ge(gate_stored[par], n * 8 + (-8 * par))
                nc.scalar.activation(gate_buf[par][:, 0:S], work_a[:], ACT.Tanh, scale=0.5
                                     ).then_inc(gate_tanh, 1)

            def step(n, par, h, first=False, second=False, last=False):
                u = n * 2 + h

                def for_others():
                    if not (isinstance(n, int) and n == 0):
                        move_lo(u - 2)
                    if h == 0 and not last:
                        split_qk(n + 1)
                    if h == 1 and not last:
                        split_v(n + 1, 1 - par, first=(isinstance(n, int) and n == 0))
                    if h == 1 and not (isinstance(n, int) and n == 0):
                        gate(n - 1, 1 - par, first=second)

                softmax(u, before_exp=for_others)
                if not first:
                    pt_high(u - 1)

            act.wait_ge(roped, PAIRS + GROUP)
            act.wait_ge(v_stored, PAIRS)
            split_qk(0, first=True)
            split_v(0, 0, first=True)
            for n in range(4):
                for h in range(2):
                    if (n, h) == (0, 1):
                        act.wait_ge(roped, PAIRS + KT)
                    step(n, n % 2, h, first=(n == 0 and h == 0), second=(n in (1, 2)))
            with by_two(act, 4, UNITS - 2) as n:
                for par in range(2):
                    for h in range(2):
                        step(n + par, par, h)
            for n in (UNITS - 2, UNITS - 1):
                for h in range(2):
                    step(n, n % 2, h, last=(n == UNITS - 1))
            move_lo(2 * UNITS - 2)
            pt_high(2 * UNITS - 1)
            gate(UNITS - 1, 1, first=False)
            move_lo(2 * UNITS - 1)

            with act.Fori(0, KT) as f:
                act.wait_ge(conv_gated, f + 1)
                copy(c_hi[:, bass.ds(f, 1), :].rearrange("p a s -> p (a s)"), work_c[:], c_hi_ready)
            act.wait_ge(tile_done, T_CO)
            act.wait_ge(attn_stored, 2 * UNITS)
            for n in range(KT):
                copy(blocks(h_hi[:, n, :]), feature_tile(n), h_hi_ready)
            with act.Fori(0, KT) as n:
                act.wait_ge(branches_added, n + 1)
                copy(c_hi[:, bass.ds(n, 1), :].rearrange("p a s -> p (a s)"), work_c[:], c_hi_ready)
            for n in range(KT):
                act.wait_ge(psum_read, T_WO + n + 1)
                nc.scalar.activation(h_hi[:, n, :], residual(n), ACT.Copy, scale=gain[:, KT + n:KT + n + 1]
                                     ).then_inc(h_hi_ready, 1)
                if n:
                    act.wait_ge(square_added, KT + n)
                nc.scalar.activation(work_c[:], residual(n), ACT.Square).then_inc(square_ready, 1)
            rms(2)
            f_base = 0
            for c, width in enumerate(CHUNKS):
                with act.Fori(0, width) as f:
                    act.wait_ge(psum_read, f * 2 + (T_UP[c] + 1))
                    nc.scalar.activation(work_b[:, 0:S], work_a[:], ACT.Tanh, scale=0.5).then_inc(silu_tanh, 1)
                    act.wait_ge(ffn_act, f + (f_base + 1))
                    copy(c_hi[:, bass.ds(f, 1), :].rearrange("p a s -> p (a s)"), work_c[:], c_hi_ready)
                f_base += width

            def final_rms(p):
                a, b = PIECES[p]
                act.wait_ge(mean_done, 3 + p)
                nc.scalar.activation(rstd[:, a:b], scores_ps[:, a:b], ACT.Sqrt, bias=eps[:]
                                     ).then_inc(rms_ready, 1)

            i = 0
            for p, (a, b) in enumerate(PIECES):
                for n in range(KT):
                    act.wait_ge(psum_read, T_DOWN[-1] + i + 1)
                    if i >= 2:
                        act.wait_ge(square_added, 2 * KT + i - 1)
                    nc.scalar.activation(final_square(i, b - a), residual(n)[:, a:b], ACT.Square
                                         ).then_inc(square_ready, 1)
                    act.wait_ge(square_ready, 2 * KT + i + 1)
                    nc.scalar.activation(residual(n)[:, a:b], residual(n)[:, a:b], ACT.Copy,
                                         scale=gain[:, 2 * KT + n:2 * KT + n + 1]).then_inc(y_scaled, 1)
                    if p > 0 and n == 2:
                        final_rms(p - 1)
                    i += 1
                act.wait_ge(square_added, 2 * KT + i)
                copy(ssq_hi[:, a:b], rstd_sq[:, a:b], ssq_split)
            final_rms(LAST_PIECE)
            a, b = PIECES[-1]
            for n in range(KT - POOL_OUT, KT):
                act.wait_ge(out_pool, pool_scaled_before(LAST_PIECE, n) + 1)
                act.dma_start(out_t[n][:, a:b], residual(n)[:, a:b]).then_inc(out_stored, 16)

        @block.vector
        def _(dve):
            V = nc.vector

            def leave_psum(out, in1, t_plus_1, slot, ps=None):
                dve.wait_ge(tile_done, t_plus_1)
                V.tensor_tensor(out, (ps or slot_ps[slot])[:], in1, ALU.mult).then_inc(psum_read, 1)

            def lo_half(out, whole, hi, done):
                return V.tensor_tensor(out, whole, hi.bitcast(F32), ALU.subtract).then_inc(done, 1)

            def add_square(k, n, src):
                dve.wait_ge(square_ready, n * KT + k + 1)
                if k == 0:
                    V.tensor_copy(rstd_sq[:], src).then_inc(square_added, 1)
                else:
                    dve.wait_ge(square_added, n * KT + k)
                    V.tensor_tensor(rstd_sq[:], rstd_sq[:], src, ALU.add).then_inc(square_added, 1)

            def norm(n):
                if n > 1:
                    dve.wait_ge(ssq_split, 2 * n - 1)
                    lo_half(ssq_lo[:], rstd_sq[:], ssq_hi[:], ssq_split)
                dve.wait_ge(rms_ready, n)
                V.reciprocal(rstd[:], rstd[:]).then_inc(rstd_ready, 1)
                dve.wait_ge(rstd_ready, n)

            dve.wait_ge(setup_done, 5)
            dve.wait_ge(table_loaded, 1)
            dve.wait_ge(gains_loaded, 16)
            for k in range(KT):
                dve.wait_ge(x_loaded[x_load_of(k)], 16)
                dve.wait_ge(h_hi_ready, k + 1)
                V.scalar_tensor_tensor(h_lo[:, k, :], residual(k), gain[:, k:k + 1],
                                       h_hi[:, k, :].bitcast(F32), ALU.mult, ALU.subtract
                                       ).then_inc(h_lo_ready, 1)
            for k in range(KT):
                add_square(k, 0, square_buf[k % 2][:, 0:S])
            dve.wait_ge(square_added, KT)
            dve.wait_ge(ssq_split, 1)
            lo_half(ssq_lo[:], rstd_sq[:], ssq_hi[:], ssq_split)
            dve.wait_ge(consts_loaded, 16 * N_CONSTS)
            V.tensor_copy(take_cur[:].rearrange("p (t k) -> p t k", t=GROUP),
                          prob[:, 0, :].unsqueeze(1).to_broadcast([P, GROUP, P])).then_inc(mask_ready, 1)
            V.tensor_copy(prev_bias[:], bias_table[:, 0:1]).then_inc(bias_set, 1)
            norm(1)
            for i in range(PAIRS):
                leave_psum(v_feature[i][:], rstd[:], T_V + i + 1, i % 2)
            V.tensor_tensor(rstd_sq[:], rstd[:], rstd[:], ALU.mult).then_inc(rstd_sq_ready, 1)

            swap = [i ^ (ROT // 2) if i < ROT else i for i in range(32)]

            def rope(i, t_plus_1, slot, dst, first=False, ps=None):
                leave_psum(work_a[:], rstd[:], t_plus_1, slot, ps)
                if not first:
                    dve.wait_ge(roped, i)
                dve.wait_ge(psum_read, t_plus_1)
                V.stream_shuffle(work_b[:, 0:S], work_a[:], swap).then_inc(swapped, 1)
                V.tensor_tensor(work_c[:], work_a[:], rope_cos[:], ALU.mult).then_inc(cos_part, 1)
                dve.wait_ge(swapped, i + 1)
                V.tensor_tensor(work_b[:, 0:S], work_b[:, 0:S], rope_sin[:], ALU.mult).then_inc(sin_part, 1)
                dve.wait_ge(cos_part, i + 1)
                dve.wait_ge(sin_part, i + 1)
                c, b = work_c[:], work_b[:, 0:S]
                if len(dst.shape) == 3:
                    c, b = blocks(c), blocks(b)
                V.tensor_tensor(dst, c, b, ALU.add).then_inc(roped, 1)

            for i in range(PAIRS):
                rope(i, T_K + i + 1, i % 2, keys[:, P + i * S:P + (i + 1) * S], first=(i == 0),
                     ps=(spare_ps, scores_ps)[i])

            def rope_q(i):
                rope(PAIRS + i, T_Q + i + 1, i % 2, feature_tile(i))

            for i in range(KT - 1):
                rope_q(i)
            dve.wait_ge(mask_ready, 1)

            def begin_softmax(u):
                dve.wait_ge(prev_copied, u + 1)
                V.tensor_scalar(prev_bias[:], bias_table[:, bass.ds(u + 1, 1)], 1.0, None, ALU.mult
                                ).then_inc(bias_set, 1)
                by_head = scores_ps[:].rearrange("p (t w k) -> p t w k", t=GROUP, w=2)
                V.copy_predicated(scores[:], take_cur[:].rearrange("p (t k) -> p t k", t=GROUP),
                                  by_head[:, :, 1, :]).then_inc(scores_merged, 1)
                dve.wait_ge(scores_merged, u + 1)
                V.tensor_reduce(row_max[:], scores[:], AX.X, ALU.max).then_inc(max_ready, 1)
                dve.wait_ge(max_ready, u + 1)
                V.scalar_tensor_tensor(top[:], row_max[:], SCALE, sink[:, bass.ds(u * GROUP, GROUP)],
                                       ALU.mult, ALU.max).then_inc(top_ready, 1)
                dve.wait_ge(top_ready, u + 1)
                V.tensor_scalar(neg_max[:], top[:], -1.0, None, ALU.mult).then_inc(shift_ready, 1)
                V.tensor_tensor(sink_arg[:], sink[:, bass.ds(u * GROUP, GROUP)], top[:], ALU.subtract
                                ).then_inc(sink_arg_ready, 1)

            def end_softmax(u):
                dve.wait_ge(exp_done, u * (GROUP + 1) + (GROUP + 1))
                V.tensor_tensor(denom[:], exp_sum[:], sink_exp[:], ALU.add).then_inc(denom_ready, 1)
                dve.wait_ge(denom_ready, u + 1)
                V.reciprocal(inv_denom[:], denom[:]).then_inc(inv_ready, 1)
                dve.wait_ge(inv_ready, u + 1)
                V.tensor_tensor(prob[:], prob[:], inv_denom[:].unsqueeze(2).to_broadcast([P, GROUP, P]),
                                ALU.mult).then_inc(probs_ready, 1)

            def mask_probs(u, first=False):
                dve.wait_ge(probs_turned, u + 1)
                if not first:
                    dve.wait_ge(pt_lo_ready, u * 2)
                by_head = turn_ps.rearrange("p (t q) -> p t q", t=GROUP)
                V.tensor_tensor(pt_cur[:], by_head, keep_cur[:].unsqueeze(1).to_broadcast([P, GROUP, P]),
                                ALU.mult).then_inc(pt_masked, 1)
                dve.wait_ge(pt_masked, u * 2 + 1)
                V.tensor_tensor(pt_prev[:], by_head, pt_cur[:], ALU.subtract).then_inc(pt_masked, 1)

            def pt_low(u):
                for i, pt in enumerate((pt_cur, pt_prev)):
                    dve.wait_ge(pt_hi_ready, u * 2 + (i + 1))
                    lo_half(pt_lo[i][:], pt[:].rearrange("p t q -> p (t q)"), pt_hi[i][:], pt_lo_ready)

            def store_attention(n, h, u):
                rows = slice(h * HEAD, (h + 1) * HEAD)
                dve.wait_ge(pv_done, u + 1)
                dve.wait_ge(lo_moved, u + 1)
                V.tensor_tensor(m[rows, bass.ds(n * (GROUP * P), GROUP * P)], attn_ps[0:HEAD, :],
                                of_lo[0:HEAD, :], ALU.add).then_inc(attn_stored, 1)

            def gate(n, par, first=False):
                if not first:
                    dve.wait_ge(gate_tanh, n)
                leave_psum(work_a[:], rstd[:], n + (T_GATE + 1), par)

            def step(n, par, h, first=0):
                u = n * 2 + h
                begin_softmax(u)
                if first != 1:
                    mask_probs(u - 1, first=(first == 2))
                if not first:
                    store_attention(n - 1, h, u - 2)
                if first != 1:
                    pt_low(u - 1)
                end_softmax(u)
                if h == 0 and first != 1:
                    gate(n - 1, 1 - par, first=(isinstance(n, int) and n == 1))

            step(0, 0, 0, first=1)
            rope_q(KT - 1)
            step(0, 0, 1, first=2)
            for h in range(2):
                step(1, 1, h)
            with by_two(dve, 2, UNITS - 2) as n:
                for par in range(2):
                    for h in range(2):
                        step(n + par, par, h)
            for n in (UNITS - 2, UNITS - 1):
                for h in range(2):
                    step(n, n % 2, h)
            last = 2 * UNITS - 1
            mask_probs(last)
            store_attention(UNITS - 1, 0, last - 1)
            pt_low(last)
            gate(UNITS - 1, 1)
            store_attention(UNITS - 1, 1, last)

            padded = work_b
            dve.wait_ge(gate_tanh, UNITS)
            dve.wait_ge(gate_stored[0], 16 * KT)
            dve.wait_ge(gate_stored[1], 16 * KT)
            V.memset(padded[:, 0:2], 0.0).then_inc(setup_done, 1)

            def conv(f, slot):
                t = f * 3 + T_CONV

                leave_psum(work_a[:], rstd_sq[:], t + 1, slot)
                dve.wait_ge(psum_read, t + 1)
                leave_psum(padded[:, 2:S + 2], work_a[:], t + 2, 1 - slot)
                dve.wait_ge(psum_read, t + 2)
                tap = lambda j: taps[:, bass.ds(f * 3 + j, 1)]
                V.tensor_scalar(work_c[:], padded[:, 2:S + 2], tap(2), None, ALU.mult).then_inc(conv_tap, 1)
                for j in (1, 0):
                    dve.wait_ge(conv_tap, f * 3 + (2 - j))
                    V.scalar_tensor_tensor(work_c[:], padded[:, j:S + j], tap(j), work_c[:],
                                           ALU.mult, ALU.add).then_inc(conv_tap, 1)
                leave_psum(work_a[:], rstd[:], t + 3, slot)
                dve.wait_ge(psum_read, t + 3)
                dve.wait_ge(conv_tap, f * 3 + 3)
                V.tensor_tensor(work_c[:], work_c[:], work_a[:], ALU.mult).then_inc(conv_gated, 1)
                dve.wait_ge(c_hi_ready, f + 1)
                lo_half(c_lo[:, bass.ds(f, 1), :].rearrange("p a s -> p (a s)"), work_c[:],
                        c_hi[:, bass.ds(f, 1), :].rearrange("p a s -> p (a s)"), c_lo_ready)
                dve.wait_ge(c_lo_ready, f + 1)

            dve.wait_ge(setup_done, 6)
            with by_two(dve, 0, KT) as f:
                conv(f, 0)
                conv(f + 1, 1)

            for n in range(KT):
                dve.wait_ge(h_hi_ready, KT + n + 1)
                lo_half(blocks(h_lo[:, n, :]), feature_tile(n), blocks(h_hi[:, n, :]), h_lo_ready)
            for n in range(KT):
                dve.wait_ge(gate_loaded[n % 2], 16 * (n // 2 + 1))
                dve.wait_ge(tile_done, T_CO + n + 1)
                dve.wait_ge(h_lo_ready, 2 * KT)
                V.scalar_tensor_tensor(feature_tile(n), blocks(reload_buf[n % 2][:, 0:S]), 1.0,
                                       blocks(slot_ps[n % 2][:]), ALU.add, ALU.mult).then_inc(psum_read, 1)
            for n in range(KT):
                g = KT + n
                dve.wait_ge(gate_loaded[g % 2], 16 * (g // 2 + 1))
                dve.wait_ge(tile_done, T_AO + n + 1)
                dve.wait_ge(c_lo_ready, KT + n)
                V.scalar_tensor_tensor(work_c[:], reload_buf[g % 2][:, 0:S], 1.0, slot_ps[n % 2][:],
                                       ALU.add, ALU.mult).then_inc(psum_read, 1)
                dve.wait_ge(psum_read, T_AO + n + 1)
                V.tensor_tensor(blocks(work_c[:]), blocks(work_c[:]), feature_tile(n), ALU.add
                                ).then_inc(branches_added, 1)
                dve.wait_ge(c_hi_ready, KT + n + 1)
                lo_half(c_lo[:, n, :], work_c[:], c_hi[:, n, :], c_lo_ready)
            for n in range(KT):
                dve.wait_ge(x_reloaded[n % 2], 16 * (n // 2 + 1))
                dve.wait_ge(tile_done, T_WO + n + 1)
                dve.wait_ge(branches_added, KT)
                V.scalar_tensor_tensor(residual(n), slot_ps[n % 2][:], 0.5, reload_buf[n % 2][:, 0:S],
                                       ALU.mult, ALU.add).then_inc(psum_read, 1)
                dve.wait_ge(h_hi_ready, 2 * KT + n + 1)
                dve.wait_ge(psum_read, T_WO + n + 1)
                V.scalar_tensor_tensor(h_lo[:, n, :], residual(n), gain[:, KT + n:KT + n + 1],
                                       h_hi[:, n, :].bitcast(F32), ALU.mult, ALU.subtract
                                       ).then_inc(h_lo_ready, 1)
                add_square(n, 1, work_c[:])
            dve.wait_ge(square_added, 2 * KT)
            norm(2)

            def ffn(c, f, f_base, gate_ps=None):
                t = f * 2 + T_UP[c]
                leave_psum(work_a[:], rstd[:], t + 1, 0, gate_ps)
                dve.wait_ge(psum_read, t + 1)
                dve.wait_ge(silu_tanh, f + (f_base + 1))
                V.scalar_tensor_tensor(work_c[:], work_b[:, 0:S], 1.0, work_a[:], ALU.add, ALU.mult
                                       ).then_inc(silu_gate, 1)
                dve.wait_ge(silu_gate, f + (f_base + 1))
                leave_psum(work_a[:], rstd[:], t + 2, 1)
                dve.wait_ge(psum_read, t + 2)
                V.tensor_tensor(work_c[:], work_c[:], work_a[:], ALU.mult).then_inc(ffn_act, 1)
                dve.wait_ge(ffn_act, f + (f_base + 1))
                dve.wait_ge(c_hi_ready, f + (2 * KT + f_base + 1))
                lo_half(c_lo[:, bass.ds(f, 1), :].rearrange("p a s -> p (a s)"), work_c[:],
                        c_hi[:, bass.ds(f, 1), :].rearrange("p a s -> p (a s)"), c_lo_ready)
                dve.wait_ge(c_lo_ready, f + (2 * KT + f_base + 1))

            f_base = 0
            for c, width in enumerate(CHUNKS):
                peeled = 2 if c == 0 else 0
                for f in range(peeled):
                    ffn(c, f, f_base, gate_ps=(None, spare_ps)[f])
                with dve.Fori(peeled, width) as f:
                    ffn(c, f, f_base)
                f_base += width
                final = c == len(CHUNKS) - 1
                if not final:
                    with by_two(dve, 0, KT) as n:
                        for j in range(2):
                            dve.wait_ge(tile_done, n + (T_DOWN[c] + j + 1))
                            acc = m[:, bass.ds(n * S + j * S, S)]
                            V.scalar_tensor_tensor(acc, slot_ps[j][:], 0.5, acc, ALU.mult, ALU.add
                                                   ).then_inc(psum_read, 1)

            def final_rstd(p, a):
                dve.wait_ge(rms_ready, 3 + p)
                V.reciprocal(rstd[:, a:a + RECIP], rstd[:, a:a + RECIP]).then_inc(rstd_ready, 1)

            i = 0
            for p, (a, b) in enumerate(PIECES):
                for n in range(KT):
                    dve.wait_ge(tile_done, T_DOWN[-1] + i + 1)
                    V.scalar_tensor_tensor(residual(n)[:, a:b], final_ps[i % 3][:, a:b], 0.5,
                                           residual(n)[:, a:b], ALU.mult, ALU.add).then_inc(psum_read, 1)
                    dve.wait_ge(square_ready, 2 * KT + i + 1)
                    if n == 0:
                        V.tensor_copy(rstd_sq[:, a:b], final_square(i, b - a)).then_inc(square_added, 1)
                    else:
                        dve.wait_ge(square_added, 2 * KT + i)
                        V.tensor_tensor(rstd_sq[:, a:b], rstd_sq[:, a:b], final_square(i, b - a), ALU.add
                                        ).then_inc(square_added, 1)
                    if p > 0:
                        first, end = PIECES[p - 1]
                        if 3 <= n < 3 + (end - first) // RECIP:
                            final_rstd(p - 1, first + (n - 3) * RECIP)
                    i += 1
                dve.wait_ge(ssq_split, 5 + 2 * p)
                lo_half(ssq_lo[:, a:b], rstd_sq[:, a:b], ssq_hi[:, a:b], ssq_split)
            a, b = PIECES[-1]
            for first in range(a, b, RECIP):
                final_rstd(LAST_PIECE, first)
            dve.wait_ge(rstd_ready, rstd_count(LAST_PIECE))
            for n in range(KT - POOL_OUT):
                dve.wait_ge(y_scaled, LAST_PIECE * KT + n + 1)
                y = residual(n)[:, a:b]
                V.tensor_tensor(y, y, rstd[:, a:b], ALU.mult).then_inc(out_dve, 1)


def shape_constants():
    f32 = np.float32
    j = np.arange(P)
    keep_cur = (j[:, None] <= j[None, :]).astype(f32)
    take_cur = (j[None, :] <= j[:, None]).astype(f32)
    bias_table = np.zeros((P, 2 * UNITS + 1), f32)
    bias_table[:, 0:-1:2 * NB] = bias_table[:, 1:-1:2 * NB] = NEG
    inv_freq = f32(500000.0) ** (-np.arange(0, ROT, 2, dtype=f32) / f32(ROT))
    angle = np.arange(S, dtype=f32)[None, :] * inv_freq[:, None].astype(f32)
    cos, sin = np.cos(angle).astype(f32), np.sin(angle).astype(f32)
    rope_cos, rope_sin = np.ones((P, S), f32), np.zeros((P, S), f32)
    for h in range(P // HEAD):
        a, half = h * HEAD, ROT // 2
        rope_cos[a:a + half] = rope_cos[a + half:a + ROT] = cos
        rope_sin[a:a + half], rope_sin[a + half:a + ROT] = -sin, sin
    return {"ident": np.eye(P, dtype=f32), "keep_cur": keep_cur, "take_cur": take_cur,
            "bias_table": bias_table, "rope_cos": rope_cos, "rope_sin": rope_sin}


def pack_weights(w_in, w_conv_out, w_attn_out, w_o, w_gate_up, w_down):
    def cols(w, first, n):
        v = w[:, first:first + n * P].reshape(-1, P, n, P)
        return v.transpose(2, 1, 0, 3)

    bounds = np.cumsum([0, D, D, D, D, N_KV * HEAD, N_KV * HEAD, D, D])
    cb, cc, cx, q, k, v, gate_c, gate_a = bounds[:-1]
    head_order = np.array([2 * GROUP * p + GROUP * e + t for p in range(PAIRS) for t in range(GROUP)
                           for e in range(2)])
    features = (head_order[:, None] * HEAD + np.arange(HEAD)[None, :]).ravel()
    conv = np.stack([cols(w_in, c, KT) for c in (cc, cx, cb)], 1).reshape(3 * KT, P, KT, P)
    parts = [cols(w_in, v, PAIRS), cols(w_in, k, PAIRS), cols(w_in[:, q:q + D][:, features], 0, KT),
             cols(w_in, gate_c, KT), cols(w_in, gate_a, KT), conv,
             cols(w_conv_out, 0, KT), cols(w_attn_out[features], 0, KT), cols(w_o, 0, KT)]
    f0 = 0
    for width in CHUNKS:
        gu = np.stack([cols(w_gate_up, f0 * P, width), cols(w_gate_up, D_FF + f0 * P, width)], 1)
        parts.append(gu.reshape(2 * width, P, KT, P))
        down = np.zeros((KT, P, KT, P), w_down.dtype)
        down[:, :, :width] = cols(w_down[f0 * P:(f0 + width) * P], 0, KT)
        parts.append(down)
        f0 += width
    return np.ascontiguousarray(np.concatenate(parts, 0).reshape(TILES, P, KT * P))


def kernel(x, g_mix, w_in, conv_w, attn_sinks, w_conv_out, w_attn_out, w_o, g_ffn, w_gate_up,
           w_down, g_final):
    import concourse.bacc as bacc
    from concourse.bass_utils import run_bass_kernel_spmd

    arr = np.asarray
    by_tile = lambda v: arr(v).reshape(-1, KT, P).transpose(2, 0, 1)
    s = arr(attn_sinks)[0].reshape(PAIRS, 1, 2, GROUP)
    s = np.broadcast_to(s, (PAIRS, NB, 2, GROUP)).reshape(1, -1)
    arrays = {
        "x_t": np.ascontiguousarray(arr(x)[0].T).reshape(KT, P, S),
        "w_stream": pack_weights(*(arr(w)[0] for w in (w_in, w_conv_out, w_attn_out, w_o, w_gate_up, w_down))),
        "gains": np.ascontiguousarray(np.concatenate(
            [by_tile(arr(g_mix)[0]), by_tile(arr(g_ffn)[0]), by_tile(arr(g_final))], 1).reshape(P, 3 * KT)),
        "conv_w": np.ascontiguousarray(by_tile(arr(conv_w)[0]).transpose(0, 2, 1).reshape(P, 3 * KT)),
        "sinks": np.ascontiguousarray(np.broadcast_to(s, (P, s.shape[1]))),
    }
    consts = shape_constants()
    nc = bacc.Bacc("TRN2", target_bir_lowering=False, num_devices=1)

    def dram(name, a):
        return nc.dram_tensor(name, a.shape, mybir.dt.from_np(a.dtype), kind="ExternalInput").ap()

    aps = {name: dram(name, a) for name, a in arrays.items()}
    const_aps = {name: dram("const_" + name, a) for name, a in consts.items()}
    out_t = nc.dram_tensor("out_t", (KT, P, S), F32, kind="ExternalOutput").ap()
    scratch = nc.dram_tensor("gate_scratch", (2 * KT, P, S), F32, kind="Internal").ap()
    block_kernel(nc, *(aps[n] for n in ("x_t", "w_stream", "gains", "conv_w", "sinks")), out_t,
                 const_aps, scratch)
    arrays.update({"const_" + name: a for name, a in consts.items()})
    r = run_bass_kernel_spmd(nc, [arrays], core_ids=[0])
    got = r.results[0]["out_t"]
    return np.ascontiguousarray(got.reshape(D, S).T).reshape(1, S, D)
```
